# Optimizing a Trainium2 kernel written in Bass

```python
import math, functools
import jax, jax.numpy as jnp
from jax import lax
import numpy as np

D_MODEL = 1024
BATCH = 1
SEQ = 128
DEPTH = 2
DEC_BATCH = 1
DEC_SEQ = 128
PAST_LEN = 128

GRID_W = 64
NA_HEADS = 8
NA_HEAD_DIM = 64
NA_WIDTH = NA_HEADS * NA_HEAD_DIM
NA_WIN_ROWS_MAX = 8
NA_WIN_COLS = 16
NA_QBLOCK_COLS = NA_WIN_COLS
NA_KBAND_COLS = 2 * NA_WIN_COLS
ROPE_BASE = 10000.0
CTX_QBLOCK = 128
SSM_HEADS = 8
SSM_HEAD_DIM = 64
SSM_INNER = SSM_HEADS * SSM_HEAD_DIM
SSM_GROUPS = 2
SSM_STATE = 64
SSM_CONV = 3
SSM_CONV_DIM = SSM_INNER + 2 * SSM_GROUPS * SSM_STATE
SSM_CHUNK = 128
GMLP_GROUPS = 4
GMLP_WIDTH = 512
GMLP_CHUNK = 128
GMLP_GROUP_DIM = GMLP_WIDTH // GMLP_GROUPS
N_BRANCHES = 3
MOE_GROUPS = 4
MOE_EXPERTS_PER_GROUP = 8
MOE_EXPERTS = MOE_GROUPS * MOE_EXPERTS_PER_GROUP
MOE_TOP_K = 2
MOE_D_FF = 256
DEEPNORM_ALPHA = (2 * DEPTH) ** 0.25
DEEPNORM_BETA = (8 * DEPTH) ** -0.25
LN_EPS = 1e-5
RMS_EPS = 1e-5
OFF_Q = 0
OFF_K = OFF_Q + NA_WIDTH
OFF_V = OFF_K + NA_WIDTH
OFF_Z = OFF_V + NA_WIDTH
OFF_XBC = OFF_Z + SSM_INNER
OFF_DT = OFF_XBC + SSM_CONV_DIM
OFF_U = OFF_DT + 2 * SSM_HEADS
OFF_GV = OFF_U + GMLP_WIDTH
OFF_GATE = OFF_GV + GMLP_WIDTH
N_IN = OFF_GATE + N_BRANCHES * D_MODEL

kernel_name = "hybrid_diffusion_prefix_step"

def layer_norm(x, g, b):
    xf = x.astype(jnp.float32)
    mu = jnp.mean(xf, -1, keepdims=True)
    var = jnp.mean(jnp.square(xf - mu), -1, keepdims=True)
    y = (xf - mu) * lax.rsqrt(var + LN_EPS)
    return (y * g.astype(jnp.float32) + b.astype(jnp.float32)).astype(x.dtype)

def rms_norm(x, g):
    xf = x.astype(jnp.float32)
    y = xf * lax.rsqrt(jnp.mean(jnp.square(xf), -1, keepdims=True) + RMS_EPS)
    return (y * g.astype(jnp.float32)).astype(x.dtype)

def to_heads(t, n_heads):
    b, l, w = t.shape
    return t.reshape(b, l, n_heads, w // n_heads).transpose(0, 2, 1, 3)

def from_heads(t):
    b, h, l, d = t.shape
    return t.transpose(0, 2, 1, 3).reshape(b, l, h * d)

def axial_rope(x):
    t = x.shape[2]
    quarter = NA_HEAD_DIM // 4
    half = NA_HEAD_DIM // 2
    freqs = ROPE_BASE ** (-jnp.arange(quarter, dtype=jnp.float32) / quarter)
    pos = jnp.arange(t)
    def rotate(xa, p):
        ang = p.astype(jnp.float32)[:, None] * freqs[None, :]
        cos = jnp.cos(ang).astype(xa.dtype)
        sin = jnp.sin(ang).astype(xa.dtype)
        x1, x2 = xa[..., :quarter], xa[..., quarter:]
        return jnp.concatenate([x1 * cos - x2 * sin, x1 * sin + x2 * cos], -1)
    return jnp.concatenate([rotate(x[..., :half], pos // GRID_W),
                            rotate(x[..., half:], pos % GRID_W)], -1)

def context_attention(q, k, v):
    b, h, l, d = q.shape
    scale = d ** -0.5
    qb = jnp.moveaxis(q.reshape(b, h, l // CTX_QBLOCK, CTX_QBLOCK, d), 2, 0)
    def block(qq):
        s = jnp.einsum('bhqd,bhkd->bhqk', qq, k).astype(jnp.float32) * scale
        p = jax.nn.softmax(s, -1).astype(v.dtype)
        return jnp.einsum('bhqk,bhkd->bhqd', p, v)
    o = lax.map(block, qb)
    return from_heads(jnp.moveaxis(o, 0, 2).reshape(b, h, l, d))

def neighbourhood_attention(q, k, v, k_ctx, v_ctx, rpb):
    b, h, t, d = q.shape
    rows = t // GRID_W
    win_r = min(NA_WIN_ROWS_MAX, rows)
    n_cb = GRID_W // NA_QBLOCK_COLS
    q = axial_rope(q)
    k = axial_rope(k)
    r = np.arange(rows)
    key_rows = np.clip(r - win_r // 2, 0, rows - win_r)[:, None] + np.arange(win_r)[None, :]
    jb = np.arange(n_cb)
    key_cols = (np.clip(jb * NA_QBLOCK_COLS - NA_WIN_COLS // 2, 0, GRID_W - NA_KBAND_COLS)[:, None]
                + np.arange(NA_KBAND_COLS)[None, :])
    q_cols = jb[:, None] * NA_QBLOCK_COLS + np.arange(NA_QBLOCK_COLS)[None, :]
    col0 = np.clip(q_cols - NA_WIN_COLS // 2, 0, GRID_W - NA_WIN_COLS)
    valid = ((key_cols[:, None, :] >= col0[:, :, None])
             & (key_cols[:, None, :] < col0[:, :, None] + NA_WIN_COLS))
    n_win = win_r * NA_KBAND_COLS
    key_idx = (key_rows[:, None, :, None] * GRID_W + key_cols[None, :, None, :]).reshape(rows, n_cb, n_win)
    dr_idx = key_rows - r[:, None] + NA_WIN_ROWS_MAX - 1
    dc_idx = np.clip(key_cols[:, None, :] - q_cols[:, :, None] + NA_WIN_COLS - 1, 0, 2 * NA_WIN_COLS - 2)
    bias = rpb[:, dr_idx[:, None, None, :, None], dc_idx[None, :, :, None, :]].astype(jnp.float32)
    bias = jnp.where(valid[None, None, :, :, None, :], bias, -jnp.inf).reshape(h, rows, n_cb, NA_QBLOCK_COLS, n_win)
    qb = q.reshape(b, h, rows, n_cb, NA_QBLOCK_COLS, d)
    kg = k[:, :, key_idx]
    vg = v[:, :, key_idx]
    scale = d ** -0.5
    s_win = jnp.einsum('bhrjqd,bhrjkd->bhrjqk', qb, kg).astype(jnp.float32) * scale + bias[None]
    s_ctx = jnp.einsum('bhrjqd,bhcd->bhrjqc', qb, k_ctx).astype(jnp.float32) * scale
    p = jax.nn.softmax(jnp.concatenate([s_win, s_ctx], -1), -1).astype(v.dtype)
    o = (jnp.einsum('bhrjqk,bhrjkd->bhrjqd', p[..., :n_win], vg)
         + jnp.einsum('bhrjqc,bhcd->bhrjqd', p[..., n_win:], v_ctx))
    return from_heads(o.reshape(b, h, t, d))

def conv_centred(x, w, bias):
    pad = SSM_CONV // 2
    y = lax.conv_general_dilated(x, w[:, None, :].astype(x.dtype), (1,), [(pad, pad)],
                                 dimension_numbers=('NWC', 'WIO', 'NWC'),
                                 feature_group_count=x.shape[-1])
    return y + bias

def ssd_scan(x, dt, a, bm, cm, h0):
    b, l, h, p = x.shape
    n = bm.shape[-1]
    nc = l // SSM_CHUNK
    xc = x.reshape(b, nc, SSM_CHUNK, h, p)
    dtc = dt.reshape(b, nc, SSM_CHUNK, h)
    bc = bm.reshape(b, nc, SSM_CHUNK, h, n)
    cc = cm.reshape(b, nc, SSM_CHUNK, h, n)
    acs = jnp.cumsum(dtc * a, axis=2)
    seg = acs[:, :, :, None, :] - acs[:, :, None, :, :]
    lower = np.tril(np.ones((SSM_CHUNK, SSM_CHUNK), dtype=bool))[None, None, :, :, None]
    decay = jnp.exp(jnp.where(lower, seg, -jnp.inf))
    xdt = xc * dtc[..., None]
    scores = jnp.einsum('bcihn,bcjhn->bcijh', cc, bc) * decay
    y_diag = jnp.einsum('bcijh,bcjhp->bcihp', scores, xdt)
    decay_to_end = jnp.exp(acs[:, :, -1:, :] - acs)
    states = jnp.einsum('bcjhn,bcjh,bcjhp->bchpn', bc, decay_to_end, xdt)
    chunk_decay = jnp.exp(acs[:, :, -1, :])
    def step(h_prev, inp):
        s, dcy = inp
        return h_prev * dcy[..., None, None] + s, h_prev
    h_fin, h_in = lax.scan(step, h0.astype(states.dtype),
                           (jnp.swapaxes(states, 0, 1), jnp.swapaxes(chunk_decay, 0, 1)))
    h_in = jnp.swapaxes(h_in, 0, 1)
    y_off = jnp.einsum('bcihn,bchpn,bcih->bcihp', cc, h_in, jnp.exp(acs))
    return (y_diag + y_off).reshape(b, l, h, p), h_fin

def ssm_branch(z, xbc, dt_raw, conv_w, conv_b, a_log, dt_bias, d_skip, norm_g, h0):
    b, l, _ = xbc.shape
    xbc = jax.nn.silu(conv_centred(xbc, conv_w, conv_b))
    gn = SSM_GROUPS * SSM_STATE
    rep = SSM_HEADS // SSM_GROUPS
    xs = xbc[..., :SSM_INNER].reshape(b, l, SSM_HEADS, SSM_HEAD_DIM)
    bm = jnp.repeat(xbc[..., SSM_INNER:SSM_INNER + gn].reshape(b, l, SSM_GROUPS, SSM_STATE), rep, axis=2)
    cm = jnp.repeat(xbc[..., SSM_INNER + gn:].reshape(b, l, SSM_GROUPS, SSM_STATE), rep, axis=2)
    dt = jax.nn.softplus(dt_raw.reshape(b, l, 2, SSM_HEADS) + dt_bias)
    a = -jnp.exp(a_log)
    y_f, h_f = ssd_scan(xs, dt[:, :, 0], a[0], bm, cm, h0[:, 0])
    y_b, h_b = ssd_scan(jnp.flip(xs, 1), jnp.flip(dt[:, :, 1], 1), a[1],
                        jnp.flip(bm, 1), jnp.flip(cm, 1), h0[:, 1])
    y = (y_f + jnp.flip(y_b, 1) + xs * d_skip[:, None]).reshape(b, l, SSM_INNER)
    y = rms_norm(y * jax.nn.silu(z), norm_g)
    return y, jnp.stack([h_f, h_b], axis=1)

def gmlp_branch(u, v, ln_g, ln_b, ws, bs):
    b, l, _ = v.shape
    u = jax.nn.gelu(u, approximate=False)
    v = layer_norm(jax.nn.gelu(v, approximate=False), ln_g, ln_b)
    vc = v.reshape(b, l // GMLP_CHUNK, GMLP_CHUNK, GMLP_GROUPS, GMLP_GROUP_DIM)
    s = jnp.einsum('gij,bcjgd->bcigd', ws, vc) + bs.T[:, :, None]
    return u * s.reshape(b, l, GMLP_WIDTH)

def token_mixer(h, attend, h0, w_in, conv_w, conv_b, a_log, dt_bias, d_skip, norm_g,
                gln_g, gln_b, ws, bs, w_branch, w_o):
    b, l, _ = h.shape
    proj = h @ w_in
    q = to_heads(proj[..., OFF_Q:OFF_K], NA_HEADS)
    k = to_heads(proj[..., OFF_K:OFF_V], NA_HEADS)
    v = to_heads(proj[..., OFF_V:OFF_Z], NA_HEADS)
    y_att = attend(q, k, v)
    y_ssm, h_fin = ssm_branch(proj[..., OFF_Z:OFF_XBC], proj[..., OFF_XBC:OFF_DT], proj[..., OFF_DT:OFF_U],
                              conv_w, conv_b, a_log, dt_bias, d_skip, norm_g, h0)
    y_gm = gmlp_branch(proj[..., OFF_U:OFF_GV], proj[..., OFF_GV:OFF_GATE], gln_g, gln_b, ws, bs)
    gates = jax.nn.sigmoid(proj[..., OFF_GATE:N_IN].reshape(b, l, N_BRANCHES, D_MODEL))
    merged = (gates[:, :, 0] * (y_att @ w_branch[0])
              + gates[:, :, 1] * (y_ssm @ w_branch[1])
              + gates[:, :, 2] * (y_gm @ w_branch[2]))
    return merged @ w_o, k, v, h_fin

def hier_moe(h, w_coarse, w_fine, w1, w3, w2):
    b, l, d = h.shape
    x = h.reshape(b * l, d)
    p_coarse = jax.nn.softmax((x @ w_coarse).astype(jnp.float32), -1)
    p_g, g_sel = lax.top_k(p_coarse, 1)
    fine = (x @ w_fine).astype(jnp.float32).reshape(-1, MOE_GROUPS, MOE_EXPERTS_PER_GROUP)
    fine_g = jnp.take_along_axis(fine, g_sel[:, :, None], axis=1)[:, 0]
    top_v, top_i = lax.top_k(fine_g, MOE_TOP_K)
    w_top = jax.nn.softmax(top_v, -1) * p_g
    expert = g_sel * MOE_EXPERTS_PER_GROUP + top_i
    gates = jnp.einsum('tk,tke->te', w_top,
                       jax.nn.one_hot(expert, MOE_EXPERTS, dtype=jnp.float32)).astype(x.dtype)
    hid = jax.nn.silu(jnp.einsum('td,edf->tef', x, w1)) * jnp.einsum('td,edf->tef', x, w3)
    y = jnp.einsum('tef,efd->td', hid * gates[:, :, None], w2)
    return y.reshape(b, l, d)

def _normal(k, shape, scale):
    return jax.random.normal(k, shape, jnp.float32) * scale

def setup_inputs(seed: int = 0) -> dict:
    key = jax.random.key(seed)
    ks = jax.random.split(key, 40)
    dt0 = jnp.exp(jax.random.uniform(ks[13], (DEPTH, 2, SSM_HEADS), jnp.float32,
                                     minval=math.log(1e-3), maxval=math.log(1e-1)))
    return {
        "x_prompt": _normal(ks[0], (BATCH, SEQ, D_MODEL), 1.0),
        "x_sample": _normal(ks[1], (DEC_BATCH, DEC_SEQ, D_MODEL), 1.0),
        "cache_k": _normal(ks[2], (DEC_BATCH, DEPTH, NA_HEADS, PAST_LEN, NA_HEAD_DIM), 1.0),
        "cache_v": _normal(ks[3], (DEC_BATCH, DEPTH, NA_HEADS, PAST_LEN, NA_HEAD_DIM), 1.0),
        "state_ssm": _normal(ks[4], (DEC_BATCH, DEPTH, 2, SSM_HEADS, SSM_HEAD_DIM, SSM_STATE), 0.5),
        "c": _normal(ks[5], (DEC_BATCH, D_MODEL), 1.0),
        "c_ctx": _normal(ks[6], (D_MODEL,), 1.0),
        "w_ada": _normal(ks[7], (DEPTH, D_MODEL, 6 * D_MODEL), D_MODEL ** -0.5),
        "b_ada": _normal(ks[8], (DEPTH, 6 * D_MODEL), 0.02),
        "w_in": _normal(ks[9], (DEPTH, D_MODEL, N_IN), D_MODEL ** -0.5),
        "na_rpb": _normal(ks[10], (DEPTH, NA_HEADS, 2 * NA_WIN_ROWS_MAX - 1, 2 * NA_WIN_COLS - 1), 0.1),
        "ssm_conv_w": _normal(ks[11], (DEPTH, SSM_CONV, SSM_CONV_DIM), SSM_CONV ** -0.5),
        "ssm_conv_b": _normal(ks[12], (DEPTH, SSM_CONV_DIM), 0.02),
        "ssm_a_log": jnp.log(jax.random.uniform(ks[14], (DEPTH, 2, SSM_HEADS), jnp.float32, minval=1.0, maxval=16.0)),
        "ssm_dt_bias": dt0 + jnp.log(-jnp.expm1(-dt0)),
        "ssm_d": 1.0 + _normal(ks[15], (DEPTH, SSM_HEADS), 0.1),
        "ssm_norm_g": 1.0 + _normal(ks[16], (DEPTH, SSM_INNER), 0.1),
        "gmlp_ln_g": 1.0 + _normal(ks[17], (DEPTH, GMLP_WIDTH), 0.1),
        "gmlp_ln_b": _normal(ks[18], (DEPTH, GMLP_WIDTH), 0.02),
        "gmlp_ws": _normal(ks[19], (DEPTH, GMLP_GROUPS, GMLP_CHUNK, GMLP_CHUNK), GMLP_CHUNK ** -0.5),
        "gmlp_bs": 1.0 + _normal(ks[20], (DEPTH, GMLP_GROUPS, GMLP_CHUNK), 0.1),
        "w_branch": _normal(ks[21], (DEPTH, N_BRANCHES, NA_WIDTH, D_MODEL), NA_WIDTH ** -0.5),
        "w_o": _normal(ks[22], (DEPTH, D_MODEL, D_MODEL), D_MODEL ** -0.5 * DEEPNORM_BETA),
        "ln_g": 1.0 + _normal(ks[23], (DEPTH, 2, D_MODEL), 0.1),
        "ln_b": _normal(ks[24], (DEPTH, 2, D_MODEL), 0.02),
        "moe_w_coarse": _normal(ks[25], (DEPTH, D_MODEL, MOE_GROUPS), D_MODEL ** -0.5),
        "moe_w_fine": _normal(ks[26], (DEPTH, D_MODEL, MOE_EXPERTS), D_MODEL ** -0.5),
        "moe_w1": _normal(ks[27], (DEPTH, MOE_EXPERTS, D_MODEL, MOE_D_FF), D_MODEL ** -0.5),
        "moe_w3": _normal(ks[28], (DEPTH, MOE_EXPERTS, D_MODEL, MOE_D_FF), D_MODEL ** -0.5),
        "moe_w2": _normal(ks[29], (DEPTH, MOE_EXPERTS, MOE_D_FF, D_MODEL), MOE_D_FF ** -0.5 * DEEPNORM_BETA),
    }

def reference(x_prompt, x_sample, cache_k, cache_v, state_ssm, c, c_ctx, w_ada, b_ada, w_in, na_rpb,
              ssm_conv_w, ssm_conv_b, ssm_a_log, ssm_dt_bias, ssm_d, ssm_norm_g, gmlp_ln_g, gmlp_ln_b,
              gmlp_ws, gmlp_bs, w_branch, w_o, ln_g, ln_b, moe_w_coarse, moe_w_fine, moe_w1, moe_w3, moe_w2):
    xp = x_prompt
    bsz = xp.shape[0]
    ks_out, vs_out, ss_out = [], [], []
    for l in range(DEPTH):
        mix_p = (w_in[l], ssm_conv_w[l], ssm_conv_b[l], ssm_a_log[l], ssm_dt_bias[l], ssm_d[l], ssm_norm_g[l],
                 gmlp_ln_g[l], gmlp_ln_b[l], gmlp_ws[l], gmlp_bs[l], w_branch[l], w_o[l])
        mod = jax.nn.silu(c_ctx) @ w_ada[l] + b_ada[l]
        sh1, sc1, g1, sh2, sc2, g2 = jnp.split(mod, 6, axis=-1)
        h0 = jnp.zeros((bsz, 2, SSM_HEADS, SSM_HEAD_DIM, SSM_STATE), xp.dtype)
        out, k, v, h_fin = token_mixer(xp * (1 + sc1) + sh1, context_attention, h0, *mix_p)
        xp = layer_norm(DEEPNORM_ALPHA * xp + g1 * out, ln_g[l, 0], ln_b[l, 0])
        ff = hier_moe(xp * (1 + sc2) + sh2, moe_w_coarse[l], moe_w_fine[l], moe_w1[l], moe_w3[l], moe_w2[l])
        xp = layer_norm(DEEPNORM_ALPHA * xp + g2 * ff, ln_g[l, 1], ln_b[l, 1])
        ks_out.append(k)
        vs_out.append(v)
        ss_out.append(h_fin)
    xs = x_sample
    for l in range(DEPTH):
        mix_p = (w_in[l], ssm_conv_w[l], ssm_conv_b[l], ssm_a_log[l], ssm_dt_bias[l], ssm_d[l], ssm_norm_g[l],
                 gmlp_ln_g[l], gmlp_ln_b[l], gmlp_ws[l], gmlp_bs[l], w_branch[l], w_o[l])
        mod = (jax.nn.silu(c) @ w_ada[l] + b_ada[l])[:, None, :]
        sh1, sc1, g1, sh2, sc2, g2 = jnp.split(mod, 6, axis=-1)
        attend = functools.partial(neighbourhood_attention, k_ctx=cache_k[:, l], v_ctx=cache_v[:, l], rpb=na_rpb[l])
        out, _, _, _ = token_mixer(xs * (1 + sc1) + sh1, attend, state_ssm[:, l], *mix_p)
        xs = layer_norm(DEEPNORM_ALPHA * xs + g1 * out, ln_g[l, 0], ln_b[l, 0])
        ff = hier_moe(xs * (1 + sc2) + sh2, moe_w_coarse[l], moe_w_fine[l], moe_w1[l], moe_w3[l], moe_w2[l])
        xs = layer_norm(DEEPNORM_ALPHA * xs + g2 * ff, ln_g[l, 1], ln_b[l, 1])
    new_cache_k = jnp.stack(ks_out, axis=1)
    new_cache_v = jnp.stack(vs_out, axis=1)
    new_state_ssm = jnp.stack(ss_out, axis=1)
    return (xp, xs, new_cache_k, new_cache_v, new_state_ssm)


_drawn_inputs = setup_inputs


def setup_inputs(seed=0):
    import zlib

    import numpy as np

    out = dict(_drawn_inputs(seed))
    spreads = {}
    factors = {'na_rpb': 6.458,
     'ssm_d': 103.284,
     'gmlp_ln_b': 8.0,
     'gmlp_ln_g': 2.672,
     'gmlp_bs': 2.753,
     'state_ssm': 4.113,
     'ssm_norm_g': 2.675}
    for name, (base, spread) in spreads.items():
        noise = np.random.default_rng([zlib.crc32(name.encode()), seed]).standard_normal(out[name].shape)
        drawn = base * np.exp(spread * noise) if base else spread * noise
        out[name] = __import__('jax').numpy.asarray(drawn.astype(out[name].dtype))
    for name, factor in factors.items():
        out[name] = (out[name] * factor).astype(out[name].dtype)
    return out
```

```python
from contextlib import ExitStack

import numpy as np

import concourse.bass as bass
from concourse import mybir

F32 = mybir.dt.float32
ALU = mybir.AluOpType
ACT = mybir.ActivationFunctionType
X = mybir.AxisListType.X

P = 128
D = 1024
DC = D // P
L = 2
ALPHA = (2 * L) ** 0.25
EPS = 1e-5
TINY = 1e-30
BIG = 1e30
GRID_W = 64
WIN = 16
HEADS = 8
HD = 64
NW = HEADS * HD
BC = NW // P
RPB_R, RPB_C = 15, 31
N_ADA = 6
E = 32
EG, EPG = 4, 8
FF = 256
HALF = NW
OFF = dict(q=0, k=512, v=1024, z=1536, xbc=2048, tail=2560, u=2832, gv=3344, gate=3856)
TAIL = 272

SLOTS = 4
SLAB = 4096
SLABS = ([("ada", s, h) for s in range(N_ADA) for h in range(2)]
         + [("q",), ("k",), ("v",), ("z",), ("xbc",), ("tail",), ("u",), ("gv",)]
         + [x for b in range(3) for x in (("gate", b, 0), ("gate", b, 1), ("branch", b))]
         + [("wo", 0), ("wo", 1), ("router",)])
MOE0 = len(SLABS)
BODY_E = 8
ITERS = E // BODY_E
BODY = [("w13", 0), ("w13", 1), ("w2", 0), ("w13", 2), ("w13", 3), ("w2", 1),
        ("w13", 4), ("w13", 5), ("w2", 2), ("w13", 6), ("w13", 7), ("w2", 3)]
assert MOE0 % SLOTS == 0 and len(BODY) % SLOTS == 0


def incs(slab):
    return 32 if slab[0] == "w13" else 16


def slot_count(slabs, k):
    return sum(incs(slabs[i]) for i in range(k % SLOTS, k + 1, SLOTS))


LOAD_A = [slot_count(SLABS, k) for k in range(MOE0)]
LOAD_B = [slot_count(BODY, k) for k in range(len(BODY))]
FULL_A = LOAD_A[-1]
FULL_B = LOAD_B[-1]
FULL_L = FULL_A + ITERS * FULL_B
USES_A, USES_B = MOE0 // SLOTS, len(BODY) // SLOTS
USES_L = USES_A + ITERS * USES_B


def make_plan():
    plan = []
    side = [4]

    def odd(name):
        plan.append((name, side[0]))
        side[0] = 4 + (side[0] - 3) % 4

    main = [0]

    def even(name):
        plan.append((name, main[0]))
        main[0] = (main[0] + 1) % 4

    for n in ("ada", "ws", "rows", "h0"):
        odd(n)
    for s in range(2):
        for h in range(2):
            even(f"x1T{s}{h}")
    for w in "qkvz":
        for s in range(2):
            even(f"{w}{s}")
    for n in ("xbc0", "xbc1", "xbc2", "dt", "u0", "u1", "gv0", "gv1"):
        even(n)
    units = [(s, g) for s in range(2) for g in range(2)]

    def gates(b):
        for h in range(2):
            for s in range(2):
                even(f"gate{b}{h}{s}")

    def branch(b):
        for s in range(2):
            odd(f"yT{b}{s}")
        for s in range(2):
            for h in range(2):
                even(f"br{b}{s}{h}")

    for i, (s, g) in enumerate(units):
        odd(f"qT{s}{g}"), odd(f"kT{s}{g}")
        if s:
            odd(f"cT{g}")
        odd(f"sw{s}{g}")
        if s:
            odd(f"sc{g}")
        even_gate = f"gate0{i // 2}{i % 2}"
        even(even_gate)
        odd(f"pw{s}{g}")
        if s:
            odd(f"pc{g}")
        odd(f"o{s}{g}")
    branch(0)
    odd("ac0"), odd("ac1")
    for s in range(2):
        odd(f"cb{s}0"), odd(f"cb{s}1")
        odd(f"xs{s}")
    odd("bt")
    odd("st0"), odd("st1")
    for n in range(8):
        odd_n = n
        plan.append((f"seg{odd_n}", 4 + n % 2))
        if n % 4 == 3:
            plan.append((f"y{n // 4}", 6 + n // 4))
    gates(1)
    branch(1)
    for s in range(2):
        odd(f"sp{s}")
    gates(2)
    branch(2)
    for s in range(2):
        for h in range(2):
            odd(f"mT{s}{h}")
    for s in range(2):
        for h in range(2):
            plan.append((f"wo{s}{h}", 2 * s + h))
    for s in range(2):
        for h in range(2):
            odd(f"g1_{s}{h}")
    for s in range(2):
        for h in range(2):
            odd(f"x2T{s}{h}")
    odd("rt")
    for s in range(2):
        for h in range(2):
            odd(f"g2_{s}{h}")
    for s in range(2):
        for h in range(2):
            plan.append((f"moe{s}{h}", 2 * s + h))
    return plan


PLAN = make_plan()
UP_BANK, HT_BANK = 4, 6
USE = {}
_uses = [0] * 8
for _name, _bank in PLAN:
    USE[_name] = (_bank, _uses[_bank])
    _uses[_bank] += 1
LOOP_USES = [0, 0, 0, 0, BODY_E, BODY_E, BODY_E // 2, BODY_E // 2]
BANK_L = [a + ITERS * b for a, b in zip(_uses, LOOP_USES)]
BANK_A = list(_uses)

CONST = dict(ident=128, upto=128, since=128, after=128, before=128, window=128, cos=64, sin=64, rev4=4, rev8=8)


def const_array():
    r = np.arange(P)
    out = {"ident": np.eye(P)}
    k, i = r[:, None], r[None, :]
    out["upto"] = k <= i
    out["since"] = k >= i
    out["after"] = k > i
    out["before"] = k < i
    qc, kc = r[:, None] % GRID_W, r[None, :] % GRID_W
    col0 = np.clip(qc - WIN // 2, 0, GRID_W - WIN)
    out["window"] = np.where((kc >= col0) & (kc < col0 + WIN), 0.0, -BIG)
    quarter = HD // 4
    freqs = np.float32(10000.0) ** (-np.arange(quarter, dtype=np.float32) / np.float32(quarter))
    cos, sin = [], []
    for pos in (r // GRID_W, r % GRID_W):
        ang = (pos.astype(np.float32)[:, None] * freqs[None, :]).astype(np.float32)
        cos += [np.cos(ang)] * 2
        sin += [-np.sin(ang), np.sin(ang)]
    out["cos"], out["sin"] = np.concatenate(cos, 1), np.concatenate(sin, 1)
    out["rev4"] = np.tile(4.0 - np.arange(4), (P, 1))
    out["rev8"] = np.tile(8.0 - np.arange(8), (P, 1))
    return np.concatenate([np.asarray(out[n], np.float32) for n in CONST], 1)


def bc(ap, axis, n):
    a = ap.unsqueeze(axis)
    shape = list(a.shape)
    shape[axis] = n
    return a.to_broadcast(shape)


def hybrid_backbone(nc, A, O):
    with ExitStack() as ctx:
        def sb(name, shape):
            return ctx.enter_context(nc.sbuf_tensor(name, shape, F32))

        def sem(name):
            return ctx.enter_context(nc.semaphore(name))

        bank = [ctx.enter_context(nc.psum_tensor(f"bank{i}", [P, 512], F32)) for i in range(8)]
        ring = sb("ring", [P, SLOTS, SLAB])
        cst = sb("cst", [P, sum(CONST.values())])
        x = sb("x", [P, 2, D])
        hT = sb("hT", [P, DC, 2 * P])
        cT = sb("cT", [P, DC, 2])
        cs = sb("cs", [P, 2, DC])
        mod = sb("mod", [P, N_ADA, DC, 2])
        bada = sb("bada", [P, N_ADA, DC])
        rows_in = sb("rows_in", [28, P])
        cols = sb("cols", [P, 28])
        hrow = sb("hrow", [P, 40])
        lnrow = sb("lnrow", [P, 2, D])
        rows3 = sb("rows3", [P, 3, NW])
        ws = sb("ws", [P, 4, P])
        wsT = sb("wsT", [P, 4, P])
        bias = sb("bias", [P, HEADS, P])
        kctx = sb("kctx", [P, HEADS, HD])
        vctx = sb("vctx", [P, HEADS, HD])
        h0 = sb("h0", [HD, 2, HEADS, HD])
        h0T = sb("h0T", [P, 2, 4, HD])
        stout = h0
        q = sb("q", [P, 2, NW])
        k = sb("k", [P, 2, NW])
        v = sb("v", [P, 2, NW])
        z = sb("z", [P, 2, NW])
        u = sb("u", [P, 2, NW])
        gv = sb("gv", [P, 2, NW])
        ropet = sb("ropet", [P, NW])
        xbc = sb("xbc", [P, 6, 2 * P])
        xs = sb("xs", [P, 2, NW])
        btok = sb("btok", [P, P])
        gate = sb("gate", [P, 2, D])
        merged = sb("merged", [P, 2, D])
        qT = sb("qT", [HD, 4, P])
        kT = sb("kT", [HD, 4, P])
        cTk = sb("cTk", [HD, 4, P])
        S = sb("S", [P, 4, 2 * P])
        pT = sb("pT", [P, 2, 4, P])
        yT = sb("yT", [P, BC, 2 * P])
        seg = sb("seg", [P, 2, 4, P])
        W = sb("W", [P, 2, 4, P])
        cbm = sb("cbm", [P, 2, 2, P])
        tmp = sb("tmp", [P, D])
        small = sb("small", [P, 32])
        stats = sb("stats", [P, 2, 12])
        mean_var = sb("mean_var", [P, 2, 2])
        root = sb("root", [P, 2])
        dtx = sb("dtx", [P, 10, 2, 16])
        acs = sb("acs", [P, 2, 32])
        wend = sb("wend", [P, 16])
        lg = sb("lg", [P, 2, 36])
        rtr = sb("rtr", [P, 2, 96])
        gates = sb("gates", [P, 2, E])
        sil = S[:, :, :].rearrange("p a b -> p (a b)")[:, 0:512].rearrange("p (s f) -> p s f", s=2)
        hid = S[:, :, :].rearrange("p a b -> p (a b)")[:, 512:1024].rearrange("p (s f) -> p s f", s=2)
        eb = S[:, :, :].rearrange("p a b -> p (a b)")[:, 0:512].rearrange("p (i t) -> p i t", i=4)
        ctS = pT
        hidT = pT[:, :, :, :]
        xw = seg[:, :, :, :].rearrange("p a b c -> p a (b c)")

        bias_rows = nc.dram_tensor("bias_rows", (L, P, HEADS, P), F32).ap()

        h0_in = h0[:, :, :, :].rearrange("p r h n -> p (r h n)").rearrange("p (r j g n) -> p r j g n", r=2, j=4, g=2)

        C, at = {}, 0
        for name, n in CONST.items():
            C[name] = cst[:, at:at + n]
            at += n

        slot_full = [sem(f"slot_full{i}") for i in range(SLOTS)]
        slot_free = [sem(f"slot_free{i}") for i in range(SLOTS)]
        full = [sem(f"full{i}") for i in range(8)]
        free = [sem(f"free{i}") for i in range(8)]
        once = sem("once")
        params = sem("params")
        bias_laid = sem("bias_laid")
        lnload = sem("lnload")
        ln_used = sem("ln_used")
        x_ready = sem("x_ready")
        c_exp = sem("c_exp")
        c_ready = sem("c_ready")
        mod_ready = sem("mod_ready")
        cols_ready = sem("cols_ready")
        ws_ready = sem("ws_ready")
        h0_ready = sem("h0_ready")
        hT_act = sem("hT_act")
        hT_dve = sem("hT_dve")
        qv_act = sem("qv_act")
        qk_dve = sem("qk_dve")
        z_ready = sem("z_ready")
        conv_done = sem("conv_done")
        xbc_ready = sem("xbc_ready")
        dt_in = sem("dt_in")
        dt_ln = sem("dt_ln")
        dtA_ready = sem("dtA_ready")
        gelu_u = sem("gelu_u")
        gelu_v = sem("gelu_v")
        gvn = sem("gvn")
        stored = sem("stored")
        stores_done = sem("stores_done")
        qkT_dve = sem("qkT_dve")
        smax = sem("smax")
        prob = sem("prob")
        pT_ready = sem("pT_ready")
        y_ready = [sem(f"y_ready{b}") for b in range(3)]
        yT_ready = sem("yT_ready")
        gate_ready = sem("gate_ready")
        merge_done = sem("merge_done")
        rem_ready = sem("rem_ready")
        rem_exp = sem("rem_exp")
        xs_ready = sem("xs_ready")
        bt_ready = sem("bt_ready")
        xw_ready = sem("xw_ready")
        st_ready = sem("st_ready")
        seg_in = sem("seg_in")
        seg_exp = sem("seg_exp")
        eb_exp = sem("eb_exp")
        W_ready = sem("W_ready")
        ct_done = sem("ct_done")
        y_sem = sem("y_sem")
        var_ready = sem("var_ready")
        root_done = sem("root_done")
        mT_ready = sem("mT_ready")
        rt_in = sem("rt_in")
        rt_exp = sem("rt_exp")
        zero_ready = sem("zero_ready")
        sil_done = sem("sil_done")
        hid_ready = sem("hid_ready")
        hidT_ready = sem("hidT_ready")
        out_ready = sem("out_ready")
        out_stored = sem("out_stored")
        pe_waited = sem("pe_waited")
        pool_waited = sem("pool_waited")

        block = ctx.enter_context(nc.Block())

        def lay(ap, l):
            return ap[bass.ds(l, 1)].squeeze(0)

        def bank_full(eng, l, name):
            b, n = USE[name]
            eng.wait_ge(full[b], l * BANK_L[b] + n + 1)
            return bank[b]

        def bank_free(eng, l, name):
            b, n = USE[name]
            eng.wait_ge(free[b], l * BANK_L[b] + n + 1)
            return bank[b]

        def fills(ins, name):
            ins.then_inc(full[USE[name][0]], 1)

        def frees(ins, name):
            ins.then_inc(free[USE[name][0]], 1)

        @block.sync
        def _(sp):
            def source(l, slab):
                kind = slab[0]
                if kind == "ada":
                    s, h = slab[1:]
                    w = lay(A["w_ada"], l).rearrange("(p c) n -> p c n", c=DC)
                    return w[:, 4 * h:4 * h + 4, s * D:(s + 1) * D]
                w = lay(A["w_in"], l).rearrange("(p c) n -> p c n", c=DC)
                if kind in OFF and kind != "gate":
                    n = TAIL if kind == "tail" else 512
                    return w[:, :, OFF[kind]:OFF[kind] + n]
                if kind == "gate":
                    o = OFF["gate"] + slab[1] * D + slab[2] * 512
                    return w[:, :, o:o + 512]
                if kind == "branch":
                    return lay(A["w_branch"], l)[slab[1]].rearrange("(p c) n -> p c n", c=BC)
                if kind == "wo":
                    w = lay(A["w_o"], l).rearrange("(p c) n -> p c n", c=DC)
                    return w[:, 4 * slab[1]:4 * slab[1] + 4, :]
                return lay(A["router"], l).rearrange("(p c) n -> p c n", c=DC)

            sp.dma_start(cst[:, :], A["consts"]).then_inc(once, 16)
            sp.dma_start(x[:, 0, :], A["x_prompt"][0]).then_inc(once, 16)
            sp.dma_start(x[:, 1, :], A["x_sample"][0]).then_inc(once, 16)
            sp.dma_start(cs[:, 0, :], A["c_ctx"].rearrange("(p c) -> p c", c=DC)).then_inc(once, 16)
            sp.dma_start(cs[:, 1, :], A["c"][0].rearrange("(p c) -> p c", c=DC)).then_inc(once, 16)
            with sp.Fori(0, L) as l:
                for i, slab in enumerate(SLABS):
                    src = source(l, slab)
                    n = src.shape[1] * src.shape[2]
                    dst = ring[:, i % SLOTS, 0:n].rearrange("p (c n) -> p c n", n=src.shape[2])
                    sp.wait_ge(slot_free[i % SLOTS], l * USES_L + i // SLOTS + 1)
                    sp.dma_start(dst, src).then_inc(slot_full[i % SLOTS], 16)
                with sp.Fori(0, ITERS) as it:
                    for i, (kind, j) in enumerate(BODY):
                        s = i % SLOTS
                        sp.wait_ge(slot_free[s], l * USES_L + it * USES_B + (USES_A + i // SLOTS + 1))
                        if kind == "w13":
                            for n, w in enumerate(("moe_w1", "moe_w3")):
                                src = lay(A[w], l)[bass.ds(it * BODY_E + j, 1)].squeeze(0)
                                sp.dma_start(ring[:, s, n * 2048:(n + 1) * 2048],
                                             src.rearrange("(p c) f -> p (c f)", c=DC)).then_inc(slot_full[s], 16)
                        else:
                            src = lay(A["moe_w2"], l)[bass.ds(it * BODY_E + 2 * j, 2)]
                            sp.dma_start(ring[:, s, :].rearrange("p (e n) -> p e n", e=2),
                                         src.rearrange("e (p c) n -> p e (c n)", c=2)).then_inc(slot_full[s], 16)
            sp.wait_ge(out_ready, 2)
            sp.dma_start(O["y_prompt"][0], x[:, 0, :]).then_inc(out_stored, 16)
            sp.dma_start(O["y_sample"][0], x[:, 1, :]).then_inc(out_stored, 16)
            sp.wait_ge(out_stored, 32)

        N_PARAM = 12

        @block.gpsimd
        def _(pool):
            pool.sem_inc(stores_done, 1)
            for n in range(L):
                for qr in range(2):
                    for kr in range(2):
                        src = bass.AP(tensor=A["na_rpb"].tensor,
                                      offset=n * HEADS * RPB_R * RPB_C + (kr - qr + 7) * RPB_C + WIN - 1,
                                      ap=[[RPB_R * RPB_C, HEADS], [-1, GRID_W], [1, GRID_W]])
                        pool.dma_start(bias_rows[n, qr * GRID_W:(qr + 1) * GRID_W, :, kr * GRID_W:(kr + 1) * GRID_W].rearrange("q h k -> h q k"),
                                       src).then_inc(bias_laid, 16)
            pool.wait_ge(bias_laid, 16 * 4 * L)
            with pool.Fori(0, L) as l:
                pool.wait_ge(ln_used, 2 * l + 1)
                pool.sem_inc(pool_waited, 1)
                pool.dma_start(bada[:, :, :], lay(A["b_ada"], l).rearrange("(s p c) -> p s c", s=N_ADA, c=DC)).then_inc(params, 16)
                pool.dma_start(rows_in[:, :], lay(A["chan_rows"], l)).then_inc(params, 16)
                pool.dma_start(hrow[:, :], lay(A["head_rows"], l).partition_broadcast(P)).then_inc(params, 16)
                pool.dma_start(rows3[:, :, :], lay(A["rows3"], l).partition_broadcast(P)).then_inc(params, 16)
                pool.dma_start(ws[:, :, :], lay(A["gmlp_ws"], l).rearrange("g i j -> i g j")).then_inc(params, 16)
                pool.dma_start(kctx[:, :, :], lay(A["cache_k"][0], l).rearrange("h t d -> t h d")).then_inc(params, 16)
                pool.dma_start(vctx[:, :, :], lay(A["cache_v"][0], l).rearrange("h t d -> t h d")).then_inc(params, 16)
                for r in range(2):
                    for g in range(2):
                        pool.dma_start(h0_in[:, r, :, g, :],
                                       lay(A["state_ssm"][0], l)[r, 4 * g:4 * g + 4].rearrange("j p n -> p j n")).then_inc(params, 16)
                pool.dma_start(bias[:, :, :], bias_rows[bass.ds(l, 1)].squeeze(0)).then_inc(params, 16)
                pool.dma_start(lnrow[:, :, :], lay(A["ln_rows"], l)[0].partition_broadcast(P)).then_inc(lnload, 16)
                pool.wait_ge(qk_dve, 3 * l + 2)
                pool.sem_inc(pool_waited, 1)
                pool.dma_start(lay(O["new_k"][0], l).rearrange("h t d -> t h d"),
                               k[:, 0, :].rearrange("t (h d) -> t h d", h=HEADS)).then_inc(stored, 16)
                pool.wait_ge(qv_act, 3 * l + 2)
                pool.sem_inc(pool_waited, 1)
                pool.dma_start(lay(O["new_v"][0], l).rearrange("h t d -> t h d"),
                               v[:, 0, :].rearrange("t (h d) -> t h d", h=HEADS)).then_inc(stored, 16)
                pool.wait_ge(st_ready, 2 * l + 2)
                pool.sem_inc(pool_waited, 1)
                pool.dma_start(lay(O["new_state"][0], l).rearrange("r h p n -> p r h n"),
                               stout[:, :, :, :]).then_inc(stored, 16)
                pool.wait_ge(ln_used, 2 * l + 2)
                pool.sem_inc(pool_waited, 1)
                pool.dma_start(lnrow[:, :, :], lay(A["ln_rows"], l)[1].partition_broadcast(P)).then_inc(lnload, 16)
                pool.wait_ge(stored, l * 48 + 48)
                pool.sem_inc(stores_done, 1)
            pool.wait_ge(stored, 16 * 3 * L)

        UNITS = [(s, g) for s in range(2) for g in range(2)]
        QKT = [2, 4, 7, 10]

        @block.tensor
        def _(pe):
            ident = C["ident"]
            owed = []

            def behind(ins):
                if owed:
                    ins.then_inc(owed.pop(), 1)
                assert not owed
                return ins

            def mm(*args, **kw):
                return behind(nc.tensor.matmul(*args, **kw))

            def turn(*args):
                return behind(nc.tensor.transpose(*args))

            def slab(l, key):
                i = SLABS.index(key)
                pe.wait_ge(slot_full[i % SLOTS], l * FULL_L + LOAD_A[i])
                return ring[:, i % SLOTS, :]

            def release(key):
                owed.append(slot_free[SLABS.index(key) % SLOTS])

            def turn4(l, name, chunks, rows=P, width=P):
                b = bank_free(pe, l, name)
                if rows != P or width != P:
                    pe.sem_inc(pe_waited, 1)
                for i, c in enumerate(chunks):
                    ins = turn(b[0:width, i * rows:(i + 1) * rows], c, ident[0:rows, 0:rows])
                fills(ins, name)

            def turn_x(l, which):
                for s in range(2):
                    xv = x[:, s, :].rearrange("t (p c) -> t c p", c=DC)
                    for h in range(2):
                        turn4(l, f"{which}{s}{h}", [xv[:, 4 * h + i, :] for i in range(4)])

            def gate_slab(l, b, h, streams=(0, 1)):
                w = slab(l, ("gate", b, h))
                wv = w.rearrange("p (c n) -> p c n", c=DC)
                for s in streams:
                    name = f"gate{b}{h}{s}"
                    t = bank_free(pe, l, name)
                    for c in range(DC):
                        ins = mm(t[:, :], hT[:, c, s * P:(s + 1) * P], wv[:, c, :], start=c == 0, stop=c == DC - 1)
                    fills(ins, name)
                    if s == 1:
                        release(("gate", b, h))

            def simple(l, key):
                w = slab(l, key)
                wv = w.rearrange("p (c n) -> p c n", c=DC)
                for s in range(2):
                    name = f"{key[0]}{s}"
                    t = bank_free(pe, l, name)
                    for c in range(DC):
                        ins = mm(t[:, :], hT[:, c, s * P:(s + 1) * P], wv[:, c, :], start=c == 0, stop=c == DC - 1)
                    fills(ins, name)
                release(key)

            def channels(l, w, name, cols0):
                t = bank_free(pe, l, name)
                for i, col in enumerate(cols0):
                    for c in range(DC):
                        ins = mm(t[:, i * 256:(i + 1) * 256], w[:, c, col:col + P], hT[:, c, :], start=c == 0, stop=c == DC - 1)
                fills(ins, name)
                return ins

            def branch(l, b, rows):
                pe.wait_ge(y_ready[b], l + 1)
                for s in range(2):
                    yv = rows[:, s, :].rearrange("t (p c) -> t c p", c=BC)
                    turn4(l, f"yT{b}{s}", [yv[:, c, :] for c in range(BC)])
                w = slab(l, ("branch", b)).rearrange("p (c n) -> p c n", c=BC)
                for s in range(2):
                    pe.wait_ge(yT_ready, l * 6 + 2 * b + s + 1)
                    for h in range(2):
                        t = bank_free(pe, l, f"br{b}{s}{h}")
                        for c in range(BC):
                            ins = mm(t[:, :], yT[:, c, s * P:(s + 1) * P], w[:, c, h * 512:(h + 1) * 512],
                                     start=c == 0, stop=c == BC - 1)
                        fills(ins, f"br{b}{s}{h}")
                release(("branch", b))

            def residual_rows(l, sec, which):
                for s in range(2):
                    for h in range(2):
                        t = bank_free(pe, l, f"{which}{s}{h}")
                        for i in range(4):
                            g = mod[:, sec, 4 * h + i, s:s + 1]
                            ins = mm(t[:, i * P:(i + 1) * P], g.to_broadcast([P, P]), ident, start=True, stop=True)
                        fills(ins, f"{which}{s}{h}")

            for s in slot_free:
                pe.sem_inc(s, 1)
            pe.wait_ge(once, 80)
            pe.wait_ge(c_ready, 1)
            with pe.Fori(0, L) as l:
                t = bank_free(pe, l, "ada")
                for sec in range(N_ADA):
                    for h in range(2):
                        w = slab(l, ("ada", sec, h)).rearrange("p (c m i) -> p c i m", c=4, i=DC)
                        for i in range(DC):
                            for c in range(4):
                                first = sec == 0 and h == 0 and i == 0 and c == 0
                                last = sec == 5 and h == 1 and i == DC - 1 and c == 3
                                o = (sec * DC + i) * 2
                                ins = mm(t[:, o:o + 2], w[:, c, i, :], cT[:, 4 * h + c, :], start=first, stop=last,
                                         skip_group_check=True)
                        release(("ada", sec, h))
                fills(ins, "ada")
                pe.wait_ge(params, (l + 1) * 16 * N_PARAM)
                turn4(l, "ws", [ws[:, g, :] for g in range(4)])
                turn4(l, "rows", [rows_in[:, :]], rows=28)
                hb = bank_free(pe, l, "h0")
                pe.sem_inc(pe_waited, 1)
                for r in range(2):
                    for j in range(4):
                        o = (r * 4 + j) * HD
                        ins = turn(hb[:, o:o + HD], h0_in[:, r, j].rearrange("p g n -> p (g n)"), ident[0:HD, 0:HD])
                fills(ins, "h0")
                pe.wait_ge(x_ready, 2 * l + 1)
                turn_x(l, "x1T")
                pe.wait_ge(hT_act, 2 * l + 1)
                pe.wait_ge(hT_dve, 2 * l + 1)
                for key in "qkvz":
                    simple(l, (key,))
                w = slab(l, ("xbc",)).rearrange("p (c n) -> p c n", c=DC)
                channels(l, w, "xbc0", (0, 128))
                channels(l, w, "xbc1", (256, 384))
                release(("xbc",))
                w = slab(l, ("tail",))[:, 0:DC * TAIL].rearrange("p (c n) -> p c n", c=DC)
                channels(l, w, "xbc2", (0, 128))
                t = bank_free(pe, l, "dt")
                for s in range(2):
                    for c in range(DC):
                        ins = mm(t[:, s * 16:s * 16 + 16], hT[:, c, s * P:(s + 1) * P], w[:, c, 256:272],
                                 start=c == 0, stop=c == DC - 1)
                fills(ins, "dt")
                release(("tail",))
                simple(l, ("u",))
                simple(l, ("gv",))

                pe.wait_ge(qv_act, 3 * l + 3)
                pe.wait_ge(qk_dve, 3 * l + 3)
                for i, (s, g) in enumerate(UNITS):
                    heads = range(4 * g, 4 * g + 4)
                    turn4(l, f"qT{s}{g}", [q[:, s, h * HD:(h + 1) * HD] for h in heads], width=HD)
                    turn4(l, f"kT{s}{g}", [k[:, s, h * HD:(h + 1) * HD] for h in heads], width=HD)
                    if s:
                        turn4(l, f"cT{g}", [kctx[:, h, :] for h in heads], width=HD)
                    pe.wait_ge(qkT_dve, l * 10 + QKT[i])
                    for name, keys in [(f"sw{s}{g}", kT)] + ([(f"sc{g}", cTk)] if s else []):
                        t = bank_free(pe, l, name)
                        for h in range(4):
                            ins = mm(t[:, h * P:(h + 1) * P], qT[:, h, :], keys[:, h, :], start=True, stop=True)
                        fills(ins, name)
                    gate_slab(l, 0, i // 2, (i % 2,))
                    pe.wait_ge(prob, l * 4 + i + 1)
                    turn4(l, f"pw{s}{g}", [S[:, h, 0:P] for h in range(4)])
                    if s:
                        turn4(l, f"pc{g}", [S[:, h, P:2 * P] for h in range(4)])
                    pe.wait_ge(pT_ready, l * 4 + i + 1)
                    t = bank_free(pe, l, f"o{s}{g}")
                    for h in range(4):
                        hh = 4 * g + h
                        ins = mm(t[:, h * HD:(h + 1) * HD], pT[:, 0, h, :], v[:, s, hh * HD:(hh + 1) * HD],
                                 start=True, stop=not s)
                        if s:
                            ins = mm(t[:, h * HD:(h + 1) * HD], pT[:, 1, h, :], vctx[:, hh, :], start=False, stop=True)
                    fills(ins, f"o{s}{g}")
                branch(l, 0, q)

                pe.wait_ge(dtA_ready, l + 1)
                for s in range(2):
                    t = bank_free(pe, l, f"ac{s}")
                    for i, m in enumerate(("upto", "since", "after", "before")):
                        r = i % 2
                        ins = mm(t[:, 8 * i:8 * i + 8], C[m], dtx[:, 9, s, 8 * r:8 * r + 8], start=True, stop=True)
                    fills(ins, f"ac{s}")
                pe.wait_ge(xbc_ready, 3 * l + 3)
                for s in range(2):
                    for g in range(2):
                        t = bank_free(pe, l, f"cb{s}{g}")
                        r = slice(g * HD, (g + 1) * HD)
                        ins = mm(t[:, 0:P], xbc[r, 4, s * P:(s + 1) * P], xbc[r, 5, s * P:(s + 1) * P], start=True, stop=True)
                        fills(ins, f"cb{s}{g}")
                    turn4(l, f"xs{s}", [xbc[:, m, s * P:(s + 1) * P] for m in range(4)])
                turn4(l, "bt", [xbc[:, 4, 0:P]])
                pe.wait_ge(bt_ready, l + 1)
                for r in range(2):
                    pe.wait_ge(xw_ready, 2 * l + r + 1)
                    t = bank_free(pe, l, f"st{r}")
                    for h in range(HEADS):
                        ins = mm(t[0:HD, h * HD:(h + 1) * HD], xw[:, r, h * HD:(h + 1) * HD],
                                 btok[:, (h // 4) * HD:(h // 4 + 1) * HD], start=True, stop=True)
                    fills(ins, f"st{r}")
                for n in range(9):
                    if n < 8:
                        s, j = n // 4, n % 4
                        t = bank_free(pe, l, f"seg{n}")
                        for i in range(4):
                            h, r = 2 * j + i // 2, i % 2
                            ins = mm(t[:, i * P:(i + 1) * P], dtx[:, 9, s, 8 * r + h:8 * r + h + 1].to_broadcast([P, P]),
                                     C["upto" if r == 0 else "since"], start=True, stop=True)
                        fills(ins, f"seg{n}")
                    if n >= 1:
                        m = n - 1
                        s, j = m // 4, m % 4
                        if m == 0:
                            pe.wait_ge(xs_ready, 2 * l + 2)
                            pe.wait_ge(h0_ready, l + 1)
                        if j == 0:
                            yb = bank_free(pe, l, f"y{s}")
                        pe.wait_ge(W_ready, 8 * l + m + 1)
                        for i in range(4):
                            h, r = 2 * j + i // 2, i % 2
                            o = yb[:, h * HD:(h + 1) * HD]
                            ins = mm(o, W[:, m % 2, i, :], xs[:, s, h * HD:(h + 1) * HD], start=r == 0, stop=r == 1 and not s)
                            if s:
                                gp = slice((h // 4) * HD, (h // 4 + 1) * HD)
                                ins = mm(o, ctS[gp, m % 2, i, :], h0T[gp, r, h % 4, :], start=False, stop=r == 1)
                        if j == 3:
                            fills(ins, f"y{s}")
                            owed.append(y_sem)
                        else:
                            ins.then_inc(y_sem, 1)
                gate_slab(l, 1, 0)
                gate_slab(l, 1, 1)
                branch(l, 1, z)

                pe.wait_ge(ws_ready, l + 1)
                for s in range(2):
                    pe.wait_ge(gvn, l + 1)
                    t = bank_free(pe, l, f"sp{s}")
                    for g in range(4):
                        ins = mm(t[:, g * P:(g + 1) * P], wsT[:, g, :], gv[:, s, g * P:(g + 1) * P], start=True, stop=True)
                    fills(ins, f"sp{s}")
                gate_slab(l, 2, 0)
                gate_slab(l, 2, 1)
                branch(l, 2, u)

                pe.wait_ge(merge_done, 3 * l + 3)
                for s in range(2):
                    mv = merged[:, s, :].rearrange("t (p c) -> t c p", c=DC)
                    for h in range(2):
                        turn4(l, f"mT{s}{h}", [mv[:, 4 * h + i, :] for i in range(4)])
                for s in range(2):
                    for h in range(2):
                        bank_free(pe, l, f"wo{s}{h}")
                pe.wait_ge(mT_ready, 4 * l + 4)
                for i in range(2):
                    w = slab(l, ("wo", i)).rearrange("p (c n) -> p c n", c=4)
                    for s in range(2):
                        for h in range(2):
                            for c in range(4):
                                ins = mm(bank[2 * s + h][:, :], hT[:, 4 * i + c, s * P:(s + 1) * P],
                                         w[:, c, h * 512:(h + 1) * 512], start=i == 0 and c == 0, stop=i == 1 and c == 3,
                                         skip_group_check=True)
                            if i == 1 and (s, h) != (1, 1):
                                fills(ins, f"wo{s}{h}")
                    if i == 0:
                        release(("wo", 0))
                    else:
                        fills(ins, "wo11")
                        release(("wo", 1))
                pe.wait_ge(mod_ready, l + 1)
                residual_rows(l, 2, "g1_")

                pe.wait_ge(x_ready, 2 * l + 2)
                turn_x(l, "x2T")
                pe.wait_ge(hT_act, 2 * l + 2)
                pe.wait_ge(hT_dve, 2 * l + 2)
                w = slab(l, ("router",))[:, 0:DC * 36].rearrange("p (c n) -> p c n", c=DC)
                t = bank_free(pe, l, "rt")
                for s in range(2):
                    for c in range(DC):
                        ins = mm(t[:, s * 36:s * 36 + 36], hT[:, c, s * P:(s + 1) * P], w[:, c, :], start=c == 0, stop=c == DC - 1)
                fills(ins, "rt")
                release(("router",))
                residual_rows(l, 5, "g2_")

                pe.wait_ge(zero_ready, l + 1)
                for s in range(2):
                    for h in range(2):
                        t = bank_free(pe, l, f"moe{s}{h}")
                        mm(t[:, :], tmp[:, 0:P], tmp[:, 0:512], start=True, stop=False, skip_group_check=True)
                with pe.Fori(0, ITERS) as it:
                    def loop_bank_free(b, n):
                        pe.wait_ge(free[b], l * BANK_L[b] + it * LOOP_USES[b] + (BANK_A[b] + n + 1))

                    def body_slab(i):
                        pe.wait_ge(slot_full[i % SLOTS], l * FULL_L + it * FULL_B + (FULL_A + LOAD_B[i]))
                        return ring[:, i % SLOTS, :]

                    def up(e, s):
                        i = BODY.index(("w13", e))
                        if s == 0:
                            body_slab(i)
                        w = ring[:, i % SLOTS, :].rearrange("p (w c f) -> p c w f", w=2, c=DC)
                        b = UP_BANK + s
                        loop_bank_free(b, e)
                        for c in range(DC):
                            ins = mm(bank[b][:, :].rearrange("p (w f) -> p w f", w=2), hT[:, c, s * P:(s + 1) * P],
                                     w[:, c], start=c == 0, stop=c == DC - 1)
                        ins.then_inc(full[b], 1)
                        if s == 1:
                            owed.append(slot_free[i % SLOTS])

                    def turn_hidden(e):
                        b = HT_BANK + e % 2
                        loop_bank_free(b, e // 2)
                        pe.wait_ge(hid_ready, l * 2 * E + it * 2 * BODY_E + (2 * e + 4))
                        for s in range(2):
                            hv = hid[:, s, :].rearrange("t (p c) -> t c p", c=2)
                            for c in range(2):
                                o = (c * 2 + s) * P
                                ins = turn(bank[b][:, o:o + P], hv[:, c, :], ident)
                        ins.then_inc(full[b], 1)

                    def down(e):
                        i = BODY.index(("w2", e // 2))
                        if e % 2 == 0:
                            body_slab(i)
                        w = ring[:, i % SLOTS, :].rearrange("p (e c n) -> p e c n", e=2, c=2)
                        pe.wait_ge(hidT_ready, l * E + it * BODY_E + (e + 1))
                        for s in range(2):
                            for h in range(2):
                                for c in range(2):
                                    ins = mm(bank[2 * s + h][:, :], hidT[:, e % 2, c * 2 + s, :],
                                             w[:, e % 2, c, h * 512:(h + 1) * 512], start=False, stop=False,
                                             skip_group_check=True)
                        if e % 2:
                            ins.then_inc(slot_free[i % SLOTS], 1)

                    up(0, 0), up(0, 1)
                    for e in range(BODY_E):
                        if e + 1 < BODY_E:
                            up(e + 1, 0)
                        turn_hidden(e)
                        if e + 1 < BODY_E:
                            up(e + 1, 1)
                        down(e)
                for s in range(2):
                    for h in range(2):
                        ins = mm(bank[2 * s + h][:, 0:2], tmp[:, 0:P], tmp[:, 0:2], start=False, stop=True, skip_group_check=True)
                        fills(ins, f"moe{s}{h}")

        @block.scalar
        def _(act):
            A_ = nc.scalar.activation
            act.wait_ge(once, 80)
            A_(tmp[:, 0:16].rearrange("p (s c) -> p s c", s=2), cs[:, :, :], ACT.Silu).then_inc(c_exp, 1)

            with act.Fori(0, L) as l:
                def modulate(sec, which, n):
                    if n == 0:
                        act.wait_ge(mod_ready, l + 1)
                    for h in range(2):
                        t = bank_full(act, l, f"{which}0{h}")
                        for i in range(4):
                            c = 4 * h + i
                            ins = A_(hT[:, c, 0:P], t[:, i * P:(i + 1) * P], ACT.Identity,
                                     bias=mod[:, sec, c, 0:1], scale=mod[:, sec + 1, c, 0:1])
                        frees(ins, f"{which}0{h}")
                    act.drain().then_inc(hT_act, 1)

                def take(name, dst, func, done, width=512, shape=None):
                    t = bank_full(act, l, name)
                    src = t[:, 0:width] if shape is None else shape(t)
                    frees(A_(dst, src, func), name)
                    if done is not None:
                        act.drain().then_inc(done, 1)

                def square_root(n):
                    act.wait_ge(var_ready, 4 * l + n + 1)
                    A_(root[:, :], root[:, :], ACT.Sqrt).then_inc(root_done, 1)

                modulate(0, "x1T", 0)
                take("q0", q[:, 0, :], ACT.Copy, qv_act)
                act.wait_ge(stores_done, l + 1)
                take("v0", v[:, 0, :], ACT.Copy, qv_act)
                take("v1", v[:, 1, :], ACT.Copy, qv_act)
                for s in range(2):
                    take(f"z{s}", z[:, s, :], ACT.Silu, z_ready)
                for m in range(3):
                    act.wait_ge(conv_done, 3 * l + m + 1)
                    A_(xbc[:, 2 * m:2 * m + 2, :], xbc[:, 2 * m:2 * m + 2, :], ACT.Silu).then_inc(xbc_ready, 1)
                for s in range(2):
                    take(f"u{s}", u[:, s, :], ACT.Gelu, gelu_u)
                for s in range(2):
                    take(f"gv{s}", gv[:, s, :], ACT.Gelu, gelu_v)
                act.wait_ge(dt_in, l + 1)
                A_(dtx[:, 2], dtx[:, 1], ACT.Exp, scale=-1.0)
                A_(hrow[:, 16:32], hrow[:, 16:32], ACT.Exp)
                act.drain()
                A_(dtx[:, 3], dtx[:, 2], ACT.Ln, bias=1.0).then_inc(dt_ln, 1)
                square_root(0)

                def gate_take(b, h, s):
                    name = f"gate{b}{h}{s}"
                    if b and h == 0 and s == 0:
                        act.wait_ge(merge_done, 3 * l + b)
                    t = bank_full(act, l, name)
                    frees(A_(gate[:, s, h * 512:(h + 1) * 512], t[:, :], ACT.Sigmoid), name)
                    act.drain().then_inc(gate_ready, 1)

                def branch_turned(b):
                    if b:
                        bank_full(act, l, f"br{b - 1}11")
                    for s in range(2):
                        name = f"yT{b}{s}"
                        t = bank_full(act, l, name)
                        frees(A_(yT[:, :, s * P:(s + 1) * P], t[:, :].rearrange("p (c t) -> p c t", c=BC), ACT.Copy), name)
                        act.drain().then_inc(yT_ready, 1)

                for i, (s, g) in enumerate(UNITS):
                    act.wait_ge(smax, l * 4 + i + 1)
                    w = 2 * P if s else P
                    A_(S[:, :, 0:w], S[:, :, 0:w], ACT.Exp, scale=HD ** -0.5)
                    act.drain().then_inc(prob, 1)
                    gate_take(0, i // 2, i % 2)
                    for n, name in enumerate([f"pw{s}{g}"] + ([f"pc{g}"] if s else [])):
                        t = bank_full(act, l, name)
                        frees(A_(pT[:, n], t[:, :].rearrange("p (h t) -> p h t", h=4), ACT.Copy), name)
                    act.drain().then_inc(pT_ready, 1)
                branch_turned(0)

                act.wait_ge(rem_ready, l + 1)
                A_(acs[:, 0, 16:32], acs[:, 0, 16:32], ACT.Exp).then_inc(rem_exp, 1)
                for s in range(2):
                    take(f"xs{s}", xs[:, s, :], ACT.Copy, xs_ready)
                for r in range(2):
                    if r == 0:
                        act.wait_ge(stores_done, l + 1)
                    t = bank_full(act, l, f"st{r}")
                    frees(A_(stout[:, r, :, :], t[0:HD, :].rearrange("p (h n) -> p h n", h=HEADS), ACT.Copy), f"st{r}")
                    act.drain().then_inc(st_ready, 1)
                for n in range(8):
                    if n >= 4:
                        t = bank_full(act, l, f"seg{n}")
                        if n >= 5:
                            act.wait_ge(ct_done, 4 * l + n - 4)
                        A_(eb[:, :, :], t[:, :].rearrange("p (i t) -> p i t", i=4), ACT.Exp)
                        act.drain().then_inc(eb_exp, 1)
                    act.wait_ge(seg_in, 8 * l + n + 1)
                    A_(seg[:, n % 2], seg[:, n % 2], ACT.Exp)
                    act.drain().then_inc(seg_exp, 1)
                for h in range(2):
                    for s in range(2):
                        gate_take(1, h, s)
                square_root(1)
                branch_turned(1)
                for h in range(2):
                    for s in range(2):
                        gate_take(2, h, s)
                branch_turned(2)
                for s in range(2):
                    for h in range(2):
                        name = f"mT{s}{h}"
                        t = bank_full(act, l, name)
                        frees(A_(hT[:, 4 * h:4 * h + 4, s * P:(s + 1) * P], t[:, :].rearrange("p (c t) -> p c t", c=4), ACT.Copy), name)
                        act.drain().then_inc(mT_ready, 1)
                square_root(2)
                modulate(3, "x2T", 1)
                for n in range(2):
                    act.wait_ge(rt_in, 2 * l + n + 1)
                    w = rtr[:, :, 0:4] if n == 0 else rtr[:, :, 40:41]
                    A_(w, w, ACT.Exp).then_inc(rt_exp, 1)
                with act.Fori(0, ITERS) as it:
                    def silu_of(e, s):
                        b = UP_BANK + s
                        act.wait_ge(full[b], l * BANK_L[b] + it * LOOP_USES[b] + (BANK_A[b] + e + 1))
                        act.wait_ge(hid_ready, l * 2 * E + it * 2 * BODY_E + (2 * e + s + 1))
                        A_(sil[:, s, :], bank[b][:, 0:FF], ACT.Silu)
                        act.drain().then_inc(sil_done, 1)

                    def turned(e):
                        b = HT_BANK + e % 2
                        act.wait_ge(full[b], l * BANK_L[b] + it * LOOP_USES[b] + (BANK_A[b] + e // 2 + 1))
                        A_(hidT[:, e % 2], bank[b][:, :].rearrange("p (c t) -> p c t", c=4), ACT.Copy).then_inc(free[b], 1)
                        act.drain().then_inc(hidT_ready, 1)

                    silu_of(0, 0), silu_of(0, 1)
                    for e in range(BODY_E):
                        turned(e)
                        if e + 1 < BODY_E:
                            silu_of(e + 1, 0), silu_of(e + 1, 1)
                square_root(3)

        @block.vector
        def _(dve):
            V = nc.vector
            drain = dve.drain

            def tt(o, a, b, op):
                return V.tensor_tensor(o, a, b, op)

            for s in free:
                dve.sem_inc(s, 1)
            dve.sem_inc(hid_ready, 2)
            dve.sem_inc(ln_used, 1)
            dve.wait_ge(once, 80)
            dve.sem_inc(x_ready, 1)
            dve.wait_ge(c_exp, 1)
            V.tensor_copy(cT[:, :, :].rearrange("p c s -> p s c"), tmp[:, 0:16].rearrange("p (s c) -> p s c", s=2)).then_inc(c_ready, 1)

            def inverse_root(l, n, var):
                V.tensor_scalar(root[:, :], var, EPS, None, ALU.add)
                drain().then_inc(var_ready, 1)
                dve.wait_ge(root_done, 4 * l + n + 1)
                V.reciprocal(root[:, :], root[:, :])
                drain()

            def layer_norm(l, n, t, width, g, b):
                blocks = width // 512
                for s in range(2):
                    for i in range(blocks):
                        V.bn_stats(stats[:, s, 6 * i:6 * i + 6], t[:, s, i * 512:(i + 1) * 512])
                drain()
                for s in range(2):
                    V.bn_aggr(mean_var[:, s, :], stats[:, s, 0:6 * blocks])
                drain()
                inverse_root(l, n, mean_var[:, :, 1])
                for s in range(2):
                    V.tensor_scalar(t[:, s, :], t[:, s, :], mean_var[:, s, 0:1], root[:, s:s + 1], ALU.subtract, ALU.mult)
                drain()
                tt(t[:, :, :], t[:, :, :], bc(g, 1, 2), ALU.mult)
                drain()
                tt(t[:, :, :], t[:, :, :], bc(b, 1, 2), ALU.add)

            with dve.Fori(0, L) as l:
                def modulate(sec, which, n):
                    for h in range(2):
                        t = bank_full(dve, l, f"{which}1{h}")
                        for i in range(4):
                            c = 4 * h + i
                            ins = V.tensor_scalar(hT[:, c, P:2 * P], t[:, i * P:(i + 1) * P], mod[:, sec + 1, c, 1:2],
                                                  mod[:, sec, c, 1:2], ALU.mult, ALU.add)
                        frees(ins, f"{which}1{h}")
                    drain().then_inc(hT_dve, 1)

                def residual_rows(which):
                    for s in range(2):
                        for h in range(2):
                            t = bank_full(dve, l, f"{which}{s}{h}")
                            gs = gate[:, s, :].rearrange("t (p c) -> t c p", c=DC)[:, 4 * h:4 * h + 4, :]
                            frees(V.tensor_copy(gs, t[:, :].rearrange("t (c p) -> t c p", c=4)), f"{which}{s}{h}")
                    drain()

                def residual(out, n):
                    dve.wait_ge(lnload, (2 * l + n + 1) * 16)
                    bank_full(dve, l, f"{out}11")
                    for s in range(2):
                        for h in range(2):
                            t = bank_full(dve, l, f"{out}{s}{h}")
                            frees(tt(tmp[:, h * 512:(h + 1) * 512], t[:, :], gate[:, s, h * 512:(h + 1) * 512], ALU.mult), f"{out}{s}{h}")
                        drain()
                        V.scalar_tensor_tensor(out=x[:, s, :], in0=x[:, s, :], scalar=ALPHA, in1=tmp[:, :], op0=ALU.mult, op1=ALU.add)
                        drain()
                    layer_norm(l, 2 + n, x, D, lnrow[:, 0, :], lnrow[:, 1, :])

                dve.wait_ge(params, (l + 1) * 16 * N_PARAM)
                t = bank_full(dve, l, "ada")
                frees(tt(mod[:, :, :, :].rearrange("p a c s -> p (a c) s"), t[:, 0:96].rearrange("p (a s) -> p a s", s=2),
                         bc(bada[:, :, :].rearrange("p a c -> p (a c)"), 2, 2), ALU.add), "ada")
                drain()
                for sec in (1, 4):
                    V.tensor_scalar(mod[:, sec], mod[:, sec], 1.0, None, ALU.add)
                drain().then_inc(mod_ready, 1)
                t = bank_full(dve, l, "rows")
                frees(V.tensor_copy(cols[:, :], t[:, 0:28]), "rows")
                t = bank_full(dve, l, "ws")
                frees(V.tensor_copy(wsT[:, :, :], t[:, :].rearrange("p (g i) -> p g i", g=4)), "ws")
                drain().then_inc(ws_ready, 1)
                t = bank_full(dve, l, "h0")
                frees(V.tensor_copy(h0T[:, :, :, :].rearrange("p r j n -> p (r j n)"), t[:, :]), "h0")
                drain().then_inc(h0_ready, 1)
                modulate(0, "x1T", 0)

                def rope(name, dst):
                    t = bank_full(dve, l, name)
                    t3 = t[:, :].rearrange("t (h d) -> t h d", h=HEADS)
                    cos = bc(C["cos"], 1, HEADS)
                    tt(dst.rearrange("t (h d) -> t h d", h=HEADS), t3, cos, ALU.mult)
                    t5 = t[:, :].rearrange("t (a b i) -> t a b i", b=2, i=16)
                    r5 = ropet[:, :].rearrange("t (a b i) -> t a b i", b=2, i=16)
                    V.tensor_copy(r5[:, :, 0, :], t5[:, :, 1, :])
                    frees(V.tensor_copy(r5[:, :, 1, :], t5[:, :, 0, :]), name)
                    drain()
                    r3 = ropet[:, :].rearrange("t (h d) -> t h d", h=HEADS)
                    tt(r3, r3, bc(C["sin"], 1, HEADS), ALU.mult)
                    drain()
                    tt(dst, dst, ropet[:, :], ALU.add)
                    drain().then_inc(qk_dve, 1)

                rope("q1", q[:, 1, :])
                dve.wait_ge(stores_done, l + 1)
                t = bank_full(dve, l, "k0")
                frees(V.tensor_copy(k[:, 0, :], t[:, :]), "k0")
                drain().then_inc(qk_dve, 1)
                rope("k1", k[:, 1, :])

                for m in range(3):
                    t = bank_full(dve, l, f"xbc{m}")
                    for i in range(2):
                        ch = 2 * m + i
                        src = t[:, i * 256:(i + 1) * 256]
                        s3 = src.rearrange("p (s t) -> p s t", s=2)
                        o3 = xbc[:, ch, :].rearrange("p (s t) -> p s t", s=2)
                        V.tensor_scalar(xbc[:, ch, :], src, cols[:, 6 + ch:7 + ch], cols[:, 18 + ch:19 + ch], ALU.mult, ALU.add)
                        drain()
                        V.scalar_tensor_tensor(out=o3[:, :, 1:P], in0=s3[:, :, 0:P - 1], scalar=cols[:, ch:ch + 1],
                                               in1=o3[:, :, 1:P], op0=ALU.mult, op1=ALU.add)
                        drain()
                        ins = V.scalar_tensor_tensor(out=o3[:, :, 0:P - 1], in0=s3[:, :, 1:P], scalar=cols[:, 12 + ch:13 + ch],
                                                     in1=o3[:, :, 0:P - 1], op0=ALU.mult, op1=ALU.add)
                    frees(ins, f"xbc{m}")
                    drain().then_inc(conv_done, 1)

                t = bank_full(dve, l, "dt")
                frees(tt(dtx[:, 0], t[:, 0:32].rearrange("p (s h) -> p s h", s=2), bc(hrow[:, 0:16], 1, 2), ALU.add), "dt")
                drain()
                V.scalar_tensor_tensor(out=dtx[:, 1], in0=dtx[:, 0], scalar=-1.0, in1=dtx[:, 0], op0=ALU.mult, op1=ALU.max)
                drain().then_inc(dt_in, 1)

                dve.wait_ge(gelu_v, 2 * l + 2)
                layer_norm(l, 0, gv, NW, rows3[:, 0, :], rows3[:, 1, :])
                drain().then_inc(gvn, 1)

                dve.wait_ge(dt_ln, l + 1)
                V.tensor_scalar(dtx[:, 4], dtx[:, 2], 1.0, None, ALU.add)
                V.tensor_scalar(dtx[:, 5], dtx[:, 3], TINY, None, ALU.add)
                V.tensor_scalar(dtx[:, 6], dtx[:, 0], 0.0, None, ALU.max)
                drain()
                V.tensor_scalar(dtx[:, 4], dtx[:, 4], -1.0, TINY, ALU.add, ALU.add)
                tt(dtx[:, 5], dtx[:, 5], dtx[:, 2], ALU.mult)
                drain()
                V.reciprocal(dtx[:, 4], dtx[:, 4])
                drain()
                tt(dtx[:, 5], dtx[:, 5], dtx[:, 4], ALU.mult)
                drain()
                tt(dtx[:, 8], dtx[:, 5], dtx[:, 6], ALU.add)
                drain()
                V.scalar_tensor_tensor(out=dtx[:, 9], in0=dtx[:, 8], scalar=-1.0, in1=bc(hrow[:, 16:32], 1, 2),
                                       op0=ALU.mult, op1=ALU.mult)
                drain().then_inc(dtA_ready, 1)

                def merge(b):
                    dve.wait_ge(gate_ready, l * 12 + 4 * b + 4)
                    for s in range(2):
                        for h in range(2):
                            t = bank_full(dve, l, f"br{b}{s}{h}")
                            hs = slice(h * 512, (h + 1) * 512)
                            if b == 0:
                                frees(tt(merged[:, s, hs], t[:, :], gate[:, s, hs], ALU.mult), f"br{b}{s}{h}")
                            else:
                                frees(tt(tmp[:, hs], t[:, :], gate[:, s, hs], ALU.mult), f"br{b}{s}{h}")
                                drain()
                                tt(merged[:, s, hs], merged[:, s, hs], tmp[:, hs], ALU.add)
                    drain().then_inc(merge_done, 1)

                for i, (s, g) in enumerate(UNITS):
                    for dst, name in [(qT, f"qT{s}{g}"), (kT, f"kT{s}{g}")] + ([(cTk, f"cT{g}")] if s else []):
                        t = bank_full(dve, l, name)
                        frees(V.tensor_copy(dst[:, :, :], t[0:HD, :].rearrange("p (h t) -> p h t", h=4)), name)
                        drain().then_inc(qkT_dve, 1)
                    w = P
                    t = bank_full(dve, l, f"sw{s}{g}")
                    t3 = t[:, :].rearrange("t (h k) -> t h k", h=4)
                    if i:
                        bank_full(dve, l, f"pc{g - 1}" if s and g else f"pw{0}{1}" if s else "pw00")
                    if s:
                        w = 2 * P
                        V.scalar_tensor_tensor(out=S[:, :, P:2 * P], in0=bias[:, 4 * g:4 * g + 4, :], scalar=HD ** 0.5,
                                               in1=bc(C["window"], 1, 4), op0=ALU.mult, op1=ALU.add)
                        drain()
                        frees(tt(S[:, :, 0:P], t3, S[:, :, P:2 * P], ALU.add), f"sw{s}{g}")
                        drain()
                        t = bank_full(dve, l, f"sc{g}")
                        frees(V.tensor_copy(S[:, :, P:2 * P], t[:, :].rearrange("t (h k) -> t h k", h=4)), f"sc{g}")
                        drain()
                        V.tensor_reduce(small[:, 20:24], S[:, :, :], X, ALU.max)
                        drain()
                        tt(S[:, :, :], S[:, :, :], bc(small[:, 20:24], 2, w), ALU.subtract)
                    else:
                        V.tensor_reduce(small[:, 20:24], t3, X, ALU.max)
                        drain()
                        frees(tt(S[:, :, 0:P], t3, bc(small[:, 20:24], 2, w), ALU.subtract), f"sw{s}{g}")
                    drain().then_inc(smax, 1)
                    dve.wait_ge(prob, l * 4 + i + 1)
                    V.tensor_reduce(small[:, 24:28], S[:, :, 0:w], X, ALU.add)
                    drain()
                    V.reciprocal(small[:, 28:32], small[:, 24:28])
                    drain()
                    t = bank_full(dve, l, f"o{s}{g}")
                    frees(tt(q[:, s, g * 256:(g + 1) * 256].rearrange("t (h d) -> t h d", h=4),
                             t[:, 0:256].rearrange("t (h d) -> t h d", h=4), bc(small[:, 28:32], 2, HD), ALU.mult), f"o{s}{g}")
                drain().then_inc(y_ready[0], 1)
                merge(0)

                for s in range(2):
                    t = bank_full(dve, l, f"ac{s}")
                    frees(V.tensor_copy(acs[:, s, :], t[:, 0:32]), f"ac{s}")
                drain().then_inc(rem_ready, 1)

                def cb_of(s):
                    for g in range(2):
                        t = bank_full(dve, l, f"cb{s}{g}")
                        frees(V.tensor_copy(cbraw[:, s, g, :], t[:, 0:P]), f"cb{s}{g}")

                cbraw = ropet[:, :].rearrange("p (s g t) -> p s g t", s=2, g=2)
                for s in range(2):
                    cb_of(s)
                t = bank_full(dve, l, "bt")
                frees(V.tensor_copy(btok[:, :], t[:, 0:P]), "bt")
                drain().then_inc(bt_ready, 1)
                dve.wait_ge(rem_exp, l + 1)
                tt(wend[:, :], acs[:, 0, 16:32], dtx[:, 8, 0, :], ALU.mult)
                drain()
                dve.wait_ge(xs_ready, 2 * l + 2)
                for r in range(2):
                    tt(xw[:, r, :].rearrange("t (h d) -> t h d", h=HEADS), xs[:, 0, :].rearrange("t (h d) -> t h d", h=HEADS),
                       bc(wend[:, 8 * r:8 * r + 8], 2, HD), ALU.mult)
                    drain().then_inc(xw_ready, 1)
                for n in range(9):
                    if n < 8:
                        s, j = n // 4, n % 4
                        if n in (0, 1):
                            bank_full(dve, l, f"st{n}")
                        if n >= 4:
                            dve.wait_ge(eb_exp, 4 * l + n - 3)
                        t = bank_full(dve, l, f"seg{n}")
                        for i in range(4):
                            h, r = 2 * j + i // 2, i % 2
                            ins = V.tensor_scalar(seg[:, n % 2, i, :], t[:, i * P:(i + 1) * P],
                                                  acs[:, s, 8 * r + h:8 * r + h + 1], 0.0, ALU.subtract, ALU.min)
                        frees(ins, f"seg{n}")
                        drain().then_inc(seg_in, 1)
                        if n >= 4:
                            gp = slice((j // 2) * HD, (j // 2 + 1) * HD)
                            dve.wait_ge(y_sem, 8 * l + n - 1)
                            tt(ctS[gp, n % 2], eb[gp], bc(xbc[gp, 5, P:2 * P], 1, 4), ALU.mult).then_inc(ct_done, 1)
                    if n >= 1:
                        m = n - 1
                        s, j = m // 4, m % 4
                        if m % 4 == 0:
                            for r, mask in enumerate(("upto", "since")):
                                tt(cbm[:, r], cbraw[:, s], bc(C[mask], 1, 2), ALU.mult)
                            drain()
                        dve.wait_ge(seg_exp, 8 * l + m + 1)
                        if m >= 2:
                            dve.wait_ge(y_sem, 8 * l + m - 1)
                        for i in range(4):
                            h, r = 2 * j + i // 2, i % 2
                            V.scalar_tensor_tensor(out=W[:, m % 2, i, :], in0=seg[:, m % 2, i, :],
                                                   scalar=dtx[:, 8, s, 8 * r + h:8 * r + h + 1], in1=cbm[:, r, h // 4, :],
                                                   op0=ALU.mult, op1=ALU.mult)
                        drain().then_inc(W_ready, 1)
                dve.wait_ge(z_ready, 2 * l + 2)
                for s in range(2):
                    y = tmp[:, 0:NW]
                    tt(y.rearrange("t (h d) -> t h d", h=HEADS), xs[:, s, :].rearrange("t (h d) -> t h d", h=HEADS),
                       bc(hrow[:, 32:40], 2, HD), ALU.mult)
                    drain()
                    t = bank_full(dve, l, f"y{s}")
                    frees(tt(y, t[:, :], y, ALU.add), f"y{s}")
                    drain()
                    tt(z[:, s, :], y, z[:, s, :], ALU.mult)
                    drain()
                    tt(tmp[:, NW:D], z[:, s, :], z[:, s, :], ALU.mult)
                    drain()
                    V.tensor_reduce(small[:, s:s + 1], tmp[:, NW:D], X, ALU.add)
                    drain()
                V.tensor_scalar(small[:, 2:4], small[:, 0:2], 1.0 / NW, None, ALU.mult)
                drain()
                inverse_root(l, 1, small[:, 2:4])
                for s in range(2):
                    V.scalar_tensor_tensor(out=z[:, s, :], in0=z[:, s, :], scalar=root[:, s:s + 1], in1=rows3[:, 2, :],
                                           op0=ALU.mult, op1=ALU.mult)
                drain().then_inc(y_ready[1], 1)
                merge(1)

                dve.wait_ge(gelu_u, 2 * l + 2)
                for s in range(2):
                    t = bank_full(dve, l, f"sp{s}")
                    for g in range(4):
                        gs = slice(g * P, (g + 1) * P)
                        ins = V.scalar_tensor_tensor(out=u[:, s, gs], in0=t[:, gs], scalar=cols[:, 24 + g:25 + g],
                                                     in1=u[:, s, gs], op0=ALU.add, op1=ALU.mult)
                    frees(ins, f"sp{s}")
                drain().then_inc(y_ready[2], 1)
                merge(2)
                residual_rows("g1_")
                residual("wo", 0)
                drain().then_inc(x_ready, 1)
                dve.sem_inc(ln_used, 1)

                V.memset(tmp[:, 0:512], 0.0)
                drain().then_inc(zero_ready, 1)
                modulate(3, "x2T", 1)
                t = bank_full(dve, l, "rt")
                frees(V.tensor_copy(lg[:, :, :], t[:, 0:72].rearrange("p (s n) -> p s n", s=2)), "rt")
                drain()

                def r_(a, b):
                    return rtr[:, :, a:b]

                V.tensor_reduce(r_(4, 5), lg[:, :, 0:4], X, ALU.max)
                drain()
                tt(r_(0, 4), lg[:, :, 0:4], r_(4, 5).to_broadcast([P, 2, 4]), ALU.subtract)
                tt(r_(8, 12), lg[:, :, 0:4], r_(4, 5).to_broadcast([P, 2, 4]), ALU.is_equal)
                drain().then_inc(rt_in, 1)

                def first(a, n, rev, m):
                    tt(r_(a, a + n), r_(a, a + n), bc(C[rev], 1, 2), ALU.mult)
                    drain()
                    V.tensor_reduce(r_(m, m + 1), r_(a, a + n), X, ALU.max)
                    drain()
                    tt(r_(a, a + n), r_(a, a + n), r_(m, m + 1).to_broadcast([P, 2, n]), ALU.is_equal)
                    drain()

                first(8, 4, "rev4", 5)
                for s in range(2):
                    tt(tmp[:, 512 + 32 * s:544 + 32 * s].rearrange("p (e g) -> p e g", g=4),
                       lg[:, s, 4:36].rearrange("p (g e) -> p e g", g=4), bc(rtr[:, s, 8:12], 1, 8), ALU.mult)
                drain()
                V.tensor_reduce(r_(16, 24), tmp[:, 512:576].rearrange("p (s e g) -> p s e g", s=2, g=4), X, ALU.add)
                drain()
                V.tensor_reduce(r_(6, 7), r_(16, 24), X, ALU.max)
                drain()
                tt(r_(24, 32), r_(16, 24), r_(6, 7).to_broadcast([P, 2, 8]), ALU.is_equal)
                drain()
                first(24, 8, "rev8", 5)
                V.scalar_tensor_tensor(out=r_(16, 24), in0=r_(24, 32), scalar=-BIG, in1=r_(16, 24), op0=ALU.mult, op1=ALU.add)
                drain()
                V.tensor_reduce(r_(7, 8), r_(16, 24), X, ALU.max)
                drain()
                tt(r_(32, 40), r_(16, 24), r_(7, 8).to_broadcast([P, 2, 8]), ALU.is_equal)
                tt(r_(40, 41), r_(7, 8), r_(6, 7), ALU.subtract)
                drain().then_inc(rt_in, 1)
                first(32, 8, "rev8", 5)
                dve.wait_ge(rt_exp, 2 * l + 2)
                V.tensor_reduce(r_(41, 42), r_(0, 4), X, ALU.add)
                V.tensor_scalar(r_(42, 43), r_(40, 41), 1.0, None, ALU.add)
                drain()
                tt(r_(43, 44), r_(41, 42), r_(42, 43), ALU.mult)
                drain()
                V.reciprocal(r_(44, 45), r_(43, 44))
                drain()
                tt(r_(45, 46), r_(44, 45), r_(40, 41), ALU.mult)
                drain()
                tt(r_(24, 32), r_(24, 32), r_(44, 45).to_broadcast([P, 2, 8]), ALU.mult)
                tt(r_(32, 40), r_(32, 40), r_(45, 46).to_broadcast([P, 2, 8]), ALU.mult)
                drain()
                tt(r_(24, 32), r_(24, 32), r_(32, 40), ALU.add)
                drain()
                for s in range(2):
                    tt(gates[:, s, :].rearrange("p (g e) -> p g e", g=4), bc(rtr[:, s, 24:32], 1, 4), bc(rtr[:, s, 8:12], 2, 8), ALU.mult)
                drain()
                residual_rows("g2_")
                with dve.Fori(0, ITERS) as it:
                    for e in range(BODY_E):
                        for s in range(2):
                            b = UP_BANK + s
                            dve.wait_ge(full[b], l * BANK_L[b] + it * LOOP_USES[b] + (BANK_A[b] + e + 1))
                            dve.wait_ge(sil_done, l * 2 * E + it * 2 * BODY_E + (2 * e + s + 1))
                            p = HT_BANK + (e - 1) % 2
                            dve.wait_ge(full[p], l * BANK_L[p] + it * LOOP_USES[p] + (BANK_A[p] + (e - 1) // 2 + 1))
                            g = gates[:, s, bass.ds(it * BODY_E + e, 1)]
                            V.scalar_tensor_tensor(out=hid[:, s, :], in0=bank[b][:, FF:2 * FF], scalar=g, in1=sil[:, s, :],
                                                   op0=ALU.mult, op1=ALU.mult).then_inc(free[b], 1)
                            drain().then_inc(hid_ready, 1)
                residual("moe", 1)
                drain().then_inc(x_ready, 1)
                dve.sem_inc(ln_used, 1)
                dve.sem_inc(out_ready, 1)


_SHAPES = dict(y_prompt=(1, P, D), y_sample=(1, P, D), new_k=(1, L, HEADS, P, HD), new_v=(1, L, HEADS, P, HD),
               new_state=(1, L, 2, HEADS, HD, HD))


def kernel(**inputs):
    import numpy as _np
    import concourse.bacc as _bacc
    from concourse import mybir as _mybir
    from concourse.bass_utils import run_bass_kernel_spmd as _run

    a = {n: _np.ascontiguousarray(w) for n, w in inputs.items()}
    a["router"] = _np.concatenate([a.pop("moe_w_coarse"), a.pop("moe_w_fine")], 2)
    a["chan_rows"] = _np.concatenate([a.pop("ssm_conv_w").reshape(L, 18, P), a.pop("ssm_conv_b").reshape(L, 6, P), a.pop("gmlp_bs")], 1)
    a["head_rows"] = _np.concatenate([a.pop("ssm_dt_bias").reshape(L, 16), a.pop("ssm_a_log").reshape(L, 16), a.pop("ssm_d")], 1)
    a["rows3"] = _np.stack([a.pop("gmlp_ln_g"), a.pop("gmlp_ln_b"), a.pop("ssm_norm_g")], 1)
    a["ln_rows"] = _np.stack([a.pop("ln_g"), a.pop("ln_b")], 2)
    a["consts"] = const_array()
    nc = _bacc.Bacc("TRN2", target_bir_lowering=False, num_devices=1)
    arrays, ins, outs = {}, {}, {}
    for name, w in a.items():
        arrays[f"in_{name}"] = w
        ins[name] = nc.dram_tensor(f"in_{name}", w.shape, _mybir.dt.from_np(w.dtype), kind="ExternalInput").ap()
    for name, shape in _SHAPES.items():
        outs[name] = nc.dram_tensor(f"out_{name}", shape, F32, kind="ExternalOutput").ap()
    hybrid_backbone(nc, ins, outs)
    r = _run(nc, [arrays], core_ids=[0])
    return tuple(r.results[0][f"out_{name}"] for name in _SHAPES)
```

```python
from contextlib import ExitStack

import numpy as np

import concourse.bass as bass
from concourse import mybir

F32 = mybir.dt.float32
F32R = mybir.dt.float32r
BF16 = mybir.dt.bfloat16
I32 = mybir.dt.int32
ALU = mybir.AluOpType
ACT = mybir.ActivationFunctionType
X = mybir.AxisListType.X

P = 128
D = 1024
DC = D // P
L = 2
ALPHA = (2 * L) ** 0.25
EPS = 1e-5
TINY = 1e-30
BIG = 1e30
GRID_W = 64
WIN = 16
HEADS = 8
HD = 64
NW = HEADS * HD
BC = NW // P
RPB_R, RPB_C = 15, 31
N_ADA = 6
E = 32
EG, EPG = 4, 8
FF = 256
HALF = NW
OFF = dict(q=0, k=512, v=1024, z=1536, xbc=2048, tail=2560, u=2832, gv=3344, gate=3856)
TAIL = 272

SLOTS = 4
PIECE = 2048
GATES = [[("gate", b, n, h) for n in range(2) for h in range(2)] for b in range(3)]
BRANCH = [[("branch", b, n) for n in range(2)] for b in range(3)]
PIECES = ([("ada", s, c) for s in range(N_ADA) for c in range(4)]
          + [("ws",)]
          + [(w, h) for w in ("q", "k", "v", "z", "xbc", "tail", "u", "gv") for h in range(2)]
          + GATES[0] + BRANCH[0] + GATES[2] + GATES[1] + BRANCH[2] + BRANCH[1]
          + [("wo", c) for c in range(4)] + [("router",)])
MOE0 = len(PIECES)
ORDER = (0, 2, 1)
FILL = [(w, h) for w in ("z", "xbc", "tail", "u", "gv") for h in range(2)] + GATES[0][:2]
SCAN_FILL = GATES[2][1:] + GATES[1]
RAW = 1 + PIECES.index(("ws",))
PARTS = 3
SPLIT = PIECES[RAW:]
BODY = [("up", 0, 0), ("up", 0, 1)]
for _e in range(1, EPG):
    BODY += [("up", _e, 0), ("up", _e, 1), ("down", _e - 1)]
BODY += [("down", EPG - 1)]
assert MOE0 % SLOTS == 0 and len(BODY) % SLOTS == 0 and len(SPLIT) % PARTS == 0 and len(BODY) % PARTS == 0
ROUNDS = 2


def incs(piece):
    return 32 if piece[0] == "up" else 16


def slot_count(pieces, k):
    return sum(incs(pieces[i]) for i in range(k % SLOTS, k + 1, SLOTS))


LOAD_A = [slot_count(PIECES, k) for k in range(MOE0)]
LOAD_B = [slot_count(BODY, k) for k in range(len(BODY))]
FULL_A = LOAD_A[-SLOTS:]
FULL_B = LOAD_B[-SLOTS:]
assert len(set(FULL_A)) == 1


WIDTH = [{"tail": 4 * TAIL, "router": DC * 36}.get(p[0], PIECE) for p in SPLIT]


class Loop:

    def __init__(self, a, b):
        self.a, self.b, self.layer = a, b, a + ROUNDS * EG * b

    def mixer(self, l, n):
        return l * self.layer + n

    def moe(self, l, rnd, g, n):
        return l * self.layer + g * self.b + (self.a + rnd * EG * self.b + n)

    def after(self, l, n):
        return l * self.layer + (ROUNDS * EG * self.b + n)


N_LOAD = [Loop(FULL_A[i], FULL_B[i]) for i in range(SLOTS)]
N_SLOT = Loop(MOE0 // SLOTS, len(BODY) // SLOTS)
N_PART = Loop(len(SPLIT) // PARTS, len(BODY) // PARTS)
N_E = Loop(0, EPG)
N_G = Loop(0, 1)


def make_plan():
    plan = []
    side = [4]

    def odd(name):
        plan.append((name, side[0]))
        side[0] = 4 + (side[0] - 3) % 4

    main = [0]

    def even(name):
        plan.append((name, main[0]))
        main[0] = (main[0] + 1) % 4

    for n in ("ada", "ws", "h0", "rows"):
        odd(n)
    for sec in range(N_ADA):
        for h in range(2):
            even(f"ada{sec}{h}")
    for s in range(2):
        for h in range(2):
            even(f"x1T{s}{h}")
    for w in "qkvz":
        for s in range(2):
            even(f"{w}{s}")
    for n in ("xbc0", "xbc1", "xbc2", "dt", "u0", "u1", "gv0", "gv1"):
        even(n)

    def gates(b):
        for h in range(2):
            for s in range(2):
                even(f"gate{b}{h}{s}")

    def branch(b):
        for s in range(2):
            odd(f"yT{b}{s}") if b == 0 else plan.append((f"yT{b}{s}", (6, 4)[b - 1] + s))
        for n in range(2):
            for s in range(2):
                even(f"br{b}{n}{s}")

    gates(0)
    for s in range(2):
        for g in range(2):
            odd(f"qT{s}{g}"), odd(f"kT{s}{g}")
            if s:
                odd(f"cT{g}")
            odd(f"sw{s}{g}")
            if s:
                odd(f"sc{g}")
            odd(f"pw{s}{g}")
            if s:
                odd(f"pc{g}")
            odd(f"o{s}{g}")
    branch(0)
    odd("sp0"), odd("sp1")
    odd("ac0"), odd("ac1")
    for s in range(2):
        odd(f"cb{s}0"), odd(f"cb{s}1")
        odd(f"xs{s}")
    odd("bt")
    odd("st0"), odd("st1")
    for n in range(8):
        odd_n = n
        plan.append((f"seg{odd_n}", 4 + n % 2))
        if n % 4 == 3:
            plan.append((f"y{n // 4}", 6 + n // 4))
    gates(2)
    gates(1)
    branch(2)
    branch(1)
    for s in range(2):
        for h in range(2):
            odd(f"mT{s}{h}")
    for s in range(2):
        for h in range(2):
            odd(f"g1_{s}{h}")
    for s in range(2):
        for h in range(2):
            plan.append((f"wo{s}{h}", 2 * s + h))
    for s in range(2):
        for h in range(2):
            odd(f"x2T{s}{h}")
    odd("rt")
    for s in range(2):
        for h in range(2):
            odd(f"x2h{s}{h}")
    for s in range(2):
        for h in range(2):
            odd(f"x2l{s}{h}")
    odd("rank")
    for s in range(2):
        for h in range(2):
            plan.append((f"moe{s}{h}", 2 * s + h))
    for s in range(2):
        for h in range(2):
            plan.append((f"g2_{s}{h}", 4 + 2 * s + h))
    return plan


PLAN = make_plan()
USE = {}
_uses = [0] * 8
for _name, _bank in PLAN:
    USE[_name] = (_bank, _uses[_bank], _name.startswith("g2_"))
    _uses[_bank] += 1
LOOP_USES = [0, 0, 0, 0, 2, 2, 1 + EPG, 2 + EPG]
AFTER = [sum(1 for n, b in PLAN if b == i and n.startswith("g2_")) for i in range(8)]
N_BANK = [Loop(a, b) for a, b in zip(_uses, LOOP_USES)]
SUM_BANK, UP_BANK, TURN_BANK = 4, 6, 7

CONST = dict(ident=128, upto=128, since=128, after=128, before=128, window=128, cos=64, sin=64, rev4=4, rev8=8, iota=128)


def const_array():
    r = np.arange(P)
    out = {"ident": np.eye(P)}
    k, i = r[:, None], r[None, :]
    out["upto"] = k <= i
    out["since"] = k >= i
    out["after"] = k > i
    out["before"] = k < i
    qc, kc = r[:, None] % GRID_W, r[None, :] % GRID_W
    col0 = np.clip(qc - WIN // 2, 0, GRID_W - WIN)
    out["window"] = np.where((kc >= col0) & (kc < col0 + WIN), 0.0, -BIG)
    quarter = HD // 4
    freqs = np.float32(10000.0) ** (-np.arange(quarter, dtype=np.float32) / np.float32(quarter))
    cos, sin = [], []
    for pos in (r // GRID_W, r % GRID_W):
        ang = (pos.astype(np.float32)[:, None] * freqs[None, :]).astype(np.float32)
        cos += [np.cos(ang)] * 2
        sin += [-np.sin(ang), np.sin(ang)]
    out["cos"], out["sin"] = np.concatenate(cos, 1), np.concatenate(sin, 1)
    out["rev4"] = np.tile(4.0 - np.arange(4), (P, 1))
    out["rev8"] = np.tile(8.0 - np.arange(8), (P, 1))
    out["iota"] = np.tile(np.arange(128.0), (P, 1))
    return np.concatenate([np.asarray(out[n], np.float32) for n in CONST], 1)


def bc(ap, axis, n):
    a = ap.unsqueeze(axis)
    shape = list(a.shape)
    shape[axis] = n
    return a.to_broadcast(shape)


def hybrid_backbone(nc, A, O):
    with ExitStack() as ctx:
        def sb(name, shape):
            return ctx.enter_context(nc.sbuf_tensor(name, shape, F32))

        def sem(name):
            return ctx.enter_context(nc.semaphore(name))

        bank = [ctx.enter_context(nc.psum_tensor(f"bank{i}", [P, 512], F32)) for i in range(8)]
        raw = sb("raw", [P, SLOTS, PIECE])
        wh = [ctx.enter_context(nc.sbuf_tensor(f"wh{i}", [P, PIECE], F32R)) for i in range(PARTS)]
        wl = [ctx.enter_context(nc.sbuf_tensor(f"wl{i}", [P, PIECE], F32R)) for i in range(PARTS)]
        cst = sb("cst", [P, sum(CONST.values())])
        x = sb("x", [P, 2, D])
        hTh = ctx.enter_context(nc.sbuf_tensor("hTh", [P, DC, 2 * P], F32R))
        hTl = ctx.enter_context(nc.sbuf_tensor("hTl", [P, DC, 2 * P], F32R))
        cT = sb("cT", [P, DC, 2])
        cs = sb("cs", [P, 2, DC])
        mod = sb("mod", [P, N_ADA, DC, 2])
        bada = sb("bada", [P, N_ADA, DC])
        rows_in = sb("rows_in", [28, P])
        cols = sb("cols", [P, 28])
        hrow = sb("hrow", [P, 40])
        rows3 = sb("rows3", [P, 3, NW])
        wsT = sb("wsT", [P, 4, P])
        h0 = sb("h0", [HD, 2, HEADS, HD])
        stout = h0
        h0T = sb("h0T", [P, 2, 4, HD])
        xbc = sb("xbc", [P, 6, 2 * P])
        btok = sb("btok", [P, P])
        tmp = sb("tmp", [P, D])
        ropet = tmp[:, 0:NW]
        small = sb("small", [P, 32])
        stats = sb("stats", [P, 2, 12])
        mean_var = sb("mean_var", [P, 2, 2])
        root = sb("root", [P, 2])
        dtx = sb("dtx", [P, 10, 2, 16])
        acs = sb("acs", [P, 2, 32])
        wend = sb("wend", [P, 16])
        lg = sb("lg", [P, 2, 36])
        rtr = sb("rtr", [P, 2, 48])
        gates = sb("gates", [P, 2, E])
        rank = sb("rank", [P, 16])
        place = sb("place", [P, 2, 2])
        gsel = sb("gsel", [P, 2, EPG])
        gg = sb("gg", [P, EPG])
        need = ctx.enter_context(nc.sbuf_tensor("need", [1, 1], I32))

        def region(name, kb, *tensors):
            start = (nc.sbuf_base + 31) // 32 * 32
            sb(name, [P, kb * 256])
            assert start + kb * 1024 == nc.sbuf_base
            return [nc.alloc_sbuf_tensor_at(n, shape, dt, offset=start + o * 1024) for n, shape, dt, o in tensors]

        (q, k, v, gate1, z, u, gv, gate, merged,
         x2h, x2l, xgh, xgl, ygh, ygl, selg, selT, hTTh, hTTl, sil, hid) = region(
            "mixer_rows", 40,
            ("q", [P, 2, NW], F32, 0),
            ("k", [P, 2, NW], F32, 4),
            ("v", [P, 2, NW], F32, 8),
            ("gate1", [P, 2, D], F32, 4),
            ("z", [P, 2, NW], F32, 12),
            ("u", [P, 2, NW], F32, 16),
            ("gv", [P, 2, NW], F32, 20),
            ("gate", [P, 2, D], F32, 24),
            ("merged", [P, 2, D], F32, 32),
            ("x2h", [P, 2, D], F32R, 0),
            ("x2l", [P, 2, D], F32R, 8),
            ("xgh", [P, DC, P], F32R, 16),
            ("xgl", [P, DC, P], F32R, 20),
            ("ygh", [P, D], F32R, 24),
            ("ygl", [P, D], F32R, 28),
            ("selg", [P, 2, P], F32R, 32),
            ("selT", [P, 2, P], F32R, 33),
            ("hTTh", [P, 2, P], F32R, 34),
            ("hTTl", [P, 2, P], F32R, 35),
            ("sil", [P, FF], F32, 36),
            ("hid", [P, FF], F32, 37))
        qT, kT, cTk, S, pT, yTh, yTl, W, eb, ctS, cbm, lnrow = region(
            "turned", 14,
            ("qT", [HD, 4, P], F32, 0), ("kT", [HD, 4, P], F32, 2), ("cTk", [HD, 4, P], F32, 4),
            ("S", [P, 4, 2 * P], F32, 6),
            ("pT", [P, 2, 4, P], F32, 10),
            ("yTh", [P, BC, 2 * P], F32R, 0), ("yTl", [P, BC, 2 * P], F32R, 4),
            ("W", [P, 2, 4, P], F32, 0), ("eb", [P, 4, P], F32, 4),
            ("ctS", [P, 2, 4, P], F32, 6),
            ("cbm", [P, 2, 2, P], F32, 10),
            ("lnrow", [P, 2, D], F32, 0))
        bias, kctx, vctx, xs, seg = region(
            "context", 8,
            ("bias", [P, HEADS, P], F32, 0),
            ("kctx", [P, HEADS, HD], F32, 4), ("vctx", [P, HEADS, HD], F32, 6),
            ("xs", [P, 2, NW], F32, 0),
            ("seg", [P, 2, 4, P], F32, 4))
        xw = seg[:, :, :, :].rearrange("p a b c -> p a (b c)")
        bias_rows = nc.dram_tensor("bias_rows", (L, P, HEADS, P), F32).ap()
        h0_in = h0[:, :, :, :].rearrange("p r h n -> p (r h n)").rearrange("p (r j g n) -> p r j g n", r=2, j=4, g=2)

        C, at = {}, 0
        for name, n in CONST.items():
            C[name] = cst[:, at:at + n]
            at += n

        slot_full = [sem(f"slot_full{i}") for i in range(SLOTS)]
        slot_free = [sem(f"slot_free{i}") for i in range(SLOTS)]
        part_high = [sem(f"part_high{i}") for i in range(PARTS)]
        part_low = [sem(f"part_low{i}") for i in range(PARTS)]
        part_free = [sem(f"part_free{i}") for i in range(PARTS)]
        full = [sem(f"full{i}") for i in range(8)]
        free = [sem(f"free{i}") for i in range(8)]
        once = sem("once")
        params = sem("params")
        bias_laid = sem("bias_laid")
        lnload = sem("lnload")
        ln_used = sem("ln_used")
        x_ready = sem("x_ready")
        c_exp = sem("c_exp")
        c_ready = sem("c_ready")
        mod_ready = sem("mod_ready")
        ada_rows = sem("ada_rows")
        ada_turned = sem("ada_turned")
        ws_ready = sem("ws_ready")
        h0_ready = sem("h0_ready")
        hT_ready = sem("hT_ready")
        qv_act = sem("qv_act")
        qk_dve = sem("qk_dve")
        z_ready = sem("z_ready")
        conv_done = sem("conv_done")
        xbc_ready = sem("xbc_ready")
        dt_in = sem("dt_in")
        dt_ln = sem("dt_ln")
        dtA_ready = sem("dtA_ready")
        gelu_u = sem("gelu_u")
        gelu_v = sem("gelu_v")
        gvn = sem("gvn")
        stored = sem("stored")
        kv_stored = sem("kv_stored")
        stores_done = sem("stores_done")
        qkT_dve = sem("qkT_dve")
        smax = sem("smax")
        prob = sem("prob")
        pT_ready = sem("pT_ready")
        y_ready = [sem(f"y_ready{b}") for b in range(3)]
        turned_high = sem("turned_high")
        turned_low = sem("turned_low")
        gate_ready = sem("gate_ready")
        merge_done = sem("merge_done")
        rem_ready = sem("rem_ready")
        rem_exp = sem("rem_exp")
        xs_ready = sem("xs_ready")
        bt_ready = sem("bt_ready")
        xw_ready = sem("xw_ready")
        st_ready = sem("st_ready")
        seg_in = sem("seg_in")
        seg_exp = sem("seg_exp")
        eb_exp = sem("eb_exp")
        W_ready = sem("W_ready")
        ct_done = sem("ct_done")
        y_sem = sem("y_sem")
        var_ready = sem("var_ready")
        root_done = sem("root_done")
        hT_full = sem("hT_full")
        hT_high = sem("hT_high")
        rt_in = sem("rt_in")
        rt_exp = sem("rt_exp")
        zero_ready = sem("zero_ready")
        x2_ready = sem("x2_ready")
        onehot_ready = sem("onehot_ready")
        need_ready = sem("need_ready")
        sel_ready = sem("sel_ready")
        selT_ready = sem("selT_ready")
        xg_act = sem("xg_act")
        xg_dve = sem("xg_dve")
        sil_done = sem("sil_done")
        hid_ready = sem("hid_ready")
        hidT_high = sem("hidT_high")
        hidT_low = sem("hidT_low")
        yg_high = sem("yg_high")
        yg_low = sem("yg_low")
        out_ready = sem("out_ready")
        out_stored = sem("out_stored")
        pe_waited = sem("pe_waited")
        pool_waited = sem("pool_waited")
        sp_waited = sem("sp_waited")
        act_waited = sem("act_waited")
        dve_waited = sem("dve_waited")

        block = ctx.enter_context(nc.Block())

        def lay(ap, l):
            return ap[bass.ds(l, 1)].squeeze(0)

        def bank_full(eng, l, name):
            b, n, after = USE[name]
            eng.wait_ge(full[b], N_BANK[b].after(l, n + 1) if after else N_BANK[b].mixer(l, n + 1))
            return bank[b]

        def bank_free(eng, l, name):
            b, n, after = USE[name]
            eng.wait_ge(free[b], N_BANK[b].after(l, n + 1) if after else N_BANK[b].mixer(l, n + 1))
            return bank[b]

        def fills(ins, name):
            ins.then_inc(full[USE[name][0]], 1)

        def frees(ins, name):
            ins.then_inc(free[USE[name][0]], 1)

        def loop_uses(b, l, rnd, g, n):
            return N_BANK[b].moe(l, rnd, g, n + 1 - AFTER[b])

        class Tally:

            def __init__(self, eng):
                self.eng, self.sems, self.counts = eng, [], []

            def __call__(self, ins, sem, n=1):
                ins.then_inc(sem, n)
                for i, s in enumerate(self.sems):
                    if s is sem:
                        self.counts[i] += n
                        return
                self.sems.append(sem)
                self.counts.append(n)

            def skip(self):
                for s, n in zip(self.sems, self.counts):
                    self.eng.sem_inc(s, EG * n)

        def rounds(eng, waited, l, group, before_skip):
            eng.sem_inc(waited, 1)
            with eng.Fori(0, EG) as g:
                group(Tally(eng), 0, g)
            eng.wait_ge(need_ready, l + 1)
            eng.sem_inc(waited, 1)
            more = eng.value_load(need[0:1, 0:1], min_val=0, max_val=1)
            tally = Tally(eng)
            with eng.If(more > 0):
                with eng.Fori(0, EG) as g:
                    group(tally, 1, g)
            with eng.Else():
                before_skip()
                tally.skip()

        @block.sync
        def _(sp):
            def source(l, piece):
                kind = piece[0]
                if kind == "ada":
                    s, c = piece[1:]
                    w = lay(A["w_ada"], l).rearrange("(p c) n -> p c n", c=DC)
                    return w[:, 2 * c:2 * c + 2, s * D:(s + 1) * D]
                if kind == "ws":
                    return lay(A["gmlp_ws"], l).rearrange("g i j -> i g j")
                w = lay(A["w_in"], l).rearrange("(p c) n -> p c n", c=DC)
                if kind in OFF and kind != "gate":
                    n = TAIL if kind == "tail" else 512
                    return w[:, 4 * piece[1]:4 * piece[1] + 4, OFF[kind]:OFF[kind] + n]
                if kind == "gate":
                    o = OFF["gate"] + piece[1] * D + piece[2] * 512
                    return w[:, 4 * piece[3]:4 * piece[3] + 4, o:o + 512]
                if kind == "branch":
                    n = piece[2]
                    return lay(A["w_branch"], l)[piece[1]].rearrange("(p c) n -> p c n", c=BC)[:, :, n * 512:(n + 1) * 512]
                if kind == "wo":
                    w = lay(A["w_o"], l).rearrange("(p c) n -> p c n", c=DC)
                    return w[:, 2 * piece[1]:2 * piece[1] + 2, :]
                return lay(A["router"], l).rearrange("(p c) n -> p c n", c=DC)

            sp.dma_start(cst[:, :], A["consts"]).then_inc(once, 16)
            sp.dma_start(x[:, 0, :], A["x_prompt"][0]).then_inc(once, 16)
            sp.dma_start(x[:, 1, :], A["x_sample"][0]).then_inc(once, 16)
            sp.dma_start(cs[:, 0, :], A["c_ctx"].rearrange("(p c) -> p c", c=DC)).then_inc(once, 16)
            sp.dma_start(cs[:, 1, :], A["c"][0].rearrange("(p c) -> p c", c=DC)).then_inc(once, 16)
            with sp.Fori(0, L) as l:
                for i, piece in enumerate(PIECES):
                    src = source(l, piece)
                    n = src.shape[1] * src.shape[2]
                    dst = raw[:, i % SLOTS, 0:n].rearrange("p (c n) -> p c n", n=src.shape[2])
                    sp.wait_ge(slot_free[i % SLOTS], N_SLOT.mixer(l, i // SLOTS + 1))
                    sp.dma_start(dst, src).then_inc(slot_full[i % SLOTS], 16)

                def load_group(tally, rnd, g):
                    for i, (kind, e, *h) in enumerate(BODY):
                        s = i % SLOTS
                        sp.wait_ge(slot_free[s], N_SLOT.moe(l, rnd, g, i // SLOTS + 1))
                        if kind == "up":
                            for n, w in enumerate(("moe_w1", "moe_w3")):
                                src = lay(A[w], l)[bass.ds(g * EPG + e, 1)].squeeze(0).rearrange("(p c) f -> p (c f)", c=DC)
                                tally(sp.dma_start(raw[:, s, n * 1024:(n + 1) * 1024],
                                                   src[:, h[0] * 1024:(h[0] + 1) * 1024]), slot_full[s], 16)
                        else:
                            src = lay(A["moe_w2"], l)[bass.ds(g * EPG + e, 1)].squeeze(0)
                            tally(sp.dma_start(raw[:, s, :], src.rearrange("(p c) n -> p (c n)", c=2)), slot_full[s], 16)

                def loads_used():
                    for s in range(SLOTS):
                        sp.wait_ge(slot_free[s], N_SLOT.moe(l, 1, 0, 1))
                    sp.sem_inc(sp_waited, 1)

                rounds(sp, sp_waited, l, load_group, loads_used)
            sp.wait_ge(out_ready, 2)
            sp.dma_start(O["y_prompt"][0], x[:, 0, :]).then_inc(out_stored, 16)
            sp.dma_start(O["y_sample"][0], x[:, 1, :]).then_inc(out_stored, 16)
            sp.wait_ge(out_stored, 32)

        N_PARAM = 11

        @block.gpsimd
        def _(pool):
            pool.sem_inc(stores_done, 1)
            for n in range(L):
                for qr in range(2):
                    for kr in range(2):
                        src = bass.AP(tensor=A["na_rpb"].tensor,
                                      offset=n * HEADS * RPB_R * RPB_C + (kr - qr + 7) * RPB_C + WIN - 1,
                                      ap=[[RPB_R * RPB_C, HEADS], [-1, GRID_W], [1, GRID_W]])
                        pool.dma_start(bias_rows[n, qr * GRID_W:(qr + 1) * GRID_W, :, kr * GRID_W:(kr + 1) * GRID_W].rearrange("q h k -> h q k"),
                                       src).then_inc(bias_laid, 16)
            pool.wait_ge(bias_laid, 16 * 4 * L)
            with pool.Fori(0, L) as l:
                pool.wait_ge(ln_used, 2 * l + 1)
                pool.sem_inc(pool_waited, 1)
                pool.dma_start(bada[:, :, :], lay(A["b_ada"], l).rearrange("(s p c) -> p s c", s=N_ADA, c=DC)).then_inc(params, 16)
                pool.dma_start(rows_in[:, :], lay(A["chan_rows"], l)).then_inc(params, 16)
                pool.dma_start(hrow[:, :], lay(A["head_rows"], l).partition_broadcast(P)).then_inc(params, 16)
                pool.dma_start(rows3[:, :, :], lay(A["rows3"], l).partition_broadcast(P)).then_inc(params, 16)
                pool.dma_start(kctx[:, :, :], lay(A["cache_k"][0], l).rearrange("h t d -> t h d")).then_inc(params, 16)
                pool.dma_start(vctx[:, :, :], lay(A["cache_v"][0], l).rearrange("h t d -> t h d")).then_inc(params, 16)
                for r in range(2):
                    for g in range(2):
                        pool.dma_start(h0_in[:, r, :, g, :],
                                       lay(A["state_ssm"][0], l)[r, 4 * g:4 * g + 4].rearrange("j p n -> p j n")).then_inc(params, 16)
                pool.dma_start(bias[:, :, :], bias_rows[bass.ds(l, 1)].squeeze(0)).then_inc(params, 16)
                pool.wait_ge(qk_dve, 3 * l + 2)
                pool.sem_inc(pool_waited, 1)
                pool.dma_start(lay(O["new_k"][0], l).rearrange("h t d -> t h d"),
                               k[:, 0, :].rearrange("t (h d) -> t h d", h=HEADS)).then_inc(stored, 16)
                pool.wait_ge(qv_act, 3 * l + 2)
                pool.sem_inc(pool_waited, 1)
                pool.dma_start(lay(O["new_v"][0], l).rearrange("h t d -> t h d"),
                               v[:, 0, :].rearrange("t (h d) -> t h d", h=HEADS)).then_inc(stored, 16)
                pool.wait_ge(stored, l * 48 + 32)
                pool.sem_inc(kv_stored, 1)
                pool.wait_ge(st_ready, 2 * l + 2)
                pool.sem_inc(pool_waited, 1)
                pool.dma_start(lay(O["new_state"][0], l).rearrange("r h p n -> p r h n"),
                               stout[:, :, :, :]).then_inc(stored, 16)
                pool.wait_ge(merge_done, 3 * l + 3)
                pool.sem_inc(pool_waited, 1)
                pool.dma_start(lnrow[:, :, :], lay(A["ln_rows"], l)[0].partition_broadcast(P)).then_inc(lnload, 16)
                pool.wait_ge(ln_used, 2 * l + 2)
                pool.sem_inc(pool_waited, 1)
                pool.dma_start(lnrow[:, :, :], lay(A["ln_rows"], l)[1].partition_broadcast(P)).then_inc(lnload, 16)
                pool.wait_ge(stored, l * 48 + 48)
                pool.sem_inc(stores_done, 1)
            pool.wait_ge(stored, 16 * 3 * L)

        UNITS = [(s, g) for s in range(2) for g in range(2)]
        QKT = [2, 4, 7, 10]

        @block.tensor
        def _(pe):
            ident = C["ident"]
            owed = []

            def behind(ins):
                if owed:
                    ins.then_inc(owed.pop(), 1)
                assert not owed
                return ins

            def mm(*args, **kw):
                return behind(nc.tensor.matmul(*args, **kw))

            def turn(*args):
                return behind(nc.tensor.transpose(*args))

            def raw_piece(l, key):
                i = PIECES.index(key)
                pe.wait_ge(slot_full[i % SLOTS], N_LOAD[i % SLOTS].mixer(l, LOAD_A[i]))
                return raw[:, i % SLOTS, :]

            def release_raw(key):
                owed.append(slot_free[PIECES.index(key) % SLOTS])

            def parts(l, key, width):
                i = SPLIT.index(key)
                pe.wait_ge(part_low[i % PARTS], N_PART.mixer(l, i // PARTS + 1))
                n = min(PIECE // width, DC) * width
                return [w[i % PARTS][:, 0:n].rearrange("p (c n) -> p c n", n=width) for w in (wh, wl)]

            def release(key):
                owed.append(part_free[SPLIT.index(key) % PARTS])

            def mm3(out, a, b, start, stop):
                mm(out, a[0], b[0], start=start, stop=False, skip_group_check=True)
                mm(out, a[0], b[1], start=False, stop=False, skip_group_check=True)
                return mm(out, a[1], b[0], start=False, stop=stop, skip_group_check=True)

            def tokens(c, s):
                return [t[:, c, s * P:(s + 1) * P] for t in (hTh, hTl)]

            def turn4(l, name, chunks, rows=P, width=P):
                b = bank_free(pe, l, name)
                if rows != P or width != P:
                    pe.sem_inc(pe_waited, 1)
                for i, c in enumerate(chunks):
                    ins = turn(b[0:width, i * rows:(i + 1) * rows], c, ident[0:rows, 0:rows])
                fills(ins, name)

            def turn_x(l, which):
                for s in range(2):
                    xv = x[:, s, :].rearrange("t (p c) -> t c p", c=DC)
                    for h in range(2):
                        turn4(l, f"{which}{s}{h}", [xv[:, 4 * h + i, :] for i in range(4)])

            def project_half(l, key, h, names):
                w = parts(l, key, 512)
                for s in range(2):
                    t = bank_free(pe, l, names[s]) if h == 0 else bank[USE[names[s]][0]]
                    for c in range(4):
                        ins = mm3(t[:, :], tokens(4 * h + c, s), [i[:, c, :] for i in w], h == 0 and c == 0, h == 1 and c == 3)
                    if h == 1:
                        fills(ins, names[s])
                release(key)

            def simple(l, w):
                for h in range(2):
                    project_half(l, (w, h), h, [f"{w}0", f"{w}1"])

            def gate_part(l, b, n, h):
                project_half(l, ("gate", b, n, h), h, [f"gate{b}{n}0", f"gate{b}{n}1"])

            def channels(l, key, h, name, width, blocks, extra=None):
                w = parts(l, key, width)
                for name, blocks in zip(name, blocks):
                    t = bank_free(pe, l, name) if h == 0 else bank[USE[name][0]]
                    for i, col in enumerate(blocks):
                        for c in range(4):
                            a = [p[:, c, col:col + P] for p in w]
                            b = [p[:, 4 * h + c, :] for p in (hTh, hTl)]
                            ins = mm3(t[:, i * 256:(i + 1) * 256], a, b, h == 0 and i == 0 and c == 0, h == 1 and c == 3)
                    if h == 1:
                        fills(ins, name)
                if extra is not None:
                    t = bank_free(pe, l, extra) if h == 0 else bank[USE[extra][0]]
                    for s in range(2):
                        for c in range(4):
                            ins = mm3(t[:, s * 16:s * 16 + 16], tokens(4 * h + c, s), [p[:, c, 256:272] for p in w],
                                      h == 0 and s == 0 and c == 0, h == 1 and c == 3)
                    if h == 1:
                        fills(ins, extra)
                release(key)

            def branch_rows(l, b, rows):
                pe.wait_ge(y_ready[b], l + 1)
                for s in range(2):
                    yv = rows[:, s, :].rearrange("t (p c) -> t c p", c=BC)
                    turn4(l, f"yT{b}{s}", [yv[:, c, :] for c in range(BC)])

            def branch(l, b):
                for n in range(2):
                    w = parts(l, ("branch", b, n), 512)
                    for s in range(2):
                        if n == 0:
                            pe.wait_ge(turned_low, l * 10 + 2 * ORDER.index(b) + s + 1)
                        t = bank_free(pe, l, f"br{b}{n}{s}")
                        for c in range(BC):
                            ins = mm3(t[:, :], [p[:, c, s * P:(s + 1) * P] for p in (yTh, yTl)], [p[:, c, :] for p in w],
                                      c == 0, c == BC - 1)
                        fills(ins, f"br{b}{n}{s}")
                    release(("branch", b, n))

            def residual_rows(l, sec, which):
                for s in range(2):
                    for h in range(2):
                        t = bank_free(pe, l, f"{which}{s}{h}")
                        for i in range(4):
                            g = mod[:, sec, 4 * h + i, s:s + 1]
                            ins = mm(t[:, i * P:(i + 1) * P], g.to_broadcast([P, P]), ident, start=True, stop=True)
                        fills(ins, f"{which}{s}{h}")

            for s in part_free:
                pe.sem_inc(s, 1)
            pe.wait_ge(once, 80)
            pe.wait_ge(c_ready, 1)
            with pe.Fori(0, L) as l:
                at = bank_free(pe, l, "ada")
                pe.sem_inc(pe_waited, 1)
                for sec in range(N_ADA + 1):
                    if sec < N_ADA:
                        rows = [bank_free(pe, l, f"ada{sec}{h}") for h in range(2)]
                        for c4 in range(4):
                            w = raw_piece(l, ("ada", sec, c4)).rearrange("p (c n) -> p c n", c=2)
                            for c in range(2):
                                for h in range(2):
                                    ins = mm(rows[h][0:2, :], cT[:, 2 * c4 + c, :], w[:, c, h * 512:(h + 1) * 512],
                                             start=c4 == 0 and c == 0, stop=c4 == 3 and c == 1)
                                    if c4 == 3 and c == 1:
                                        fills(ins, f"ada{sec}{h}")
                            release_raw(("ada", sec, c4))
                    if sec:
                        pe.wait_ge(ada_rows, l * N_ADA + sec)
                        pe.sem_inc(pe_waited, 1)
                        rv = merged[0:2, (sec - 1) % 2, :].rearrange("s (p c) -> s c p", c=DC)
                        for c in range(DC):
                            o = ((sec - 1) * DC + c) * 2
                            ins = turn(at[:, o:o + 2], rv[:, c, :], ident[0:2, 0:2])
                        if sec < N_ADA:
                            ins.then_inc(ada_turned, 1)
                fills(ins, "ada")
                pe.wait_ge(params, (l + 1) * 16 * N_PARAM)
                ws = raw_piece(l, ("ws",))
                turn4(l, "ws", [ws[:, g * P:(g + 1) * P] for g in range(4)])
                release_raw(("ws",))
                hb = bank_free(pe, l, "h0")
                pe.sem_inc(pe_waited, 1)
                for r in range(2):
                    for j in range(4):
                        o = (r * 4 + j) * HD
                        ins = turn(hb[:, o:o + HD], h0_in[:, r, j].rearrange("p g n -> p (g n)"), ident[0:HD, 0:HD])
                fills(ins, "h0")
                turn4(l, "rows", [rows_in[:, :]], rows=28)
                pe.wait_ge(x_ready, 2 * l + 1)
                turn_x(l, "x1T")
                pe.wait_ge(hT_ready, 2 * l + 1)
                for key in "qkv":
                    simple(l, key)

                def fill(key):
                    if key[0] == "gate":
                        gate_part(l, *key[1:])
                    elif key[0] == "xbc":
                        channels(l, key, key[1], ("xbc0", "xbc1"), 512, ((0, 128), (256, 384)))
                    elif key[0] == "tail":
                        channels(l, key, key[1], ("xbc2",), TAIL, ((0, 128),), extra="dt")
                    else:
                        project_half(l, key, key[1], [f"{key[0]}0", f"{key[0]}1"])

                pe.wait_ge(qv_act, 3 * l + 3)
                pe.wait_ge(qk_dve, 3 * l + 3)
                for i, (s, g) in enumerate(UNITS):
                    heads = range(4 * g, 4 * g + 4)
                    turn4(l, f"qT{s}{g}", [q[:, s, h * HD:(h + 1) * HD] for h in heads], width=HD)
                    turn4(l, f"kT{s}{g}", [k[:, s, h * HD:(h + 1) * HD] for h in heads], width=HD)
                    if s:
                        turn4(l, f"cT{g}", [kctx[:, h, :] for h in heads], width=HD)
                    fill(FILL[3 * i])
                    pe.wait_ge(qkT_dve, l * 10 + QKT[i])
                    for name, keys in [(f"sw{s}{g}", kT)] + ([(f"sc{g}", cTk)] if s else []):
                        t = bank_free(pe, l, name)
                        for h in range(4):
                            ins = mm(t[:, h * P:(h + 1) * P], qT[:, h, :], keys[:, h, :], start=True, stop=True)
                        fills(ins, name)
                    fill(FILL[3 * i + 1])
                    pe.wait_ge(prob, l * 4 + i + 1)
                    turn4(l, f"pw{s}{g}", [S[:, h, 0:P] for h in range(4)])
                    if s:
                        turn4(l, f"pc{g}", [S[:, h, P:2 * P] for h in range(4)])
                    fill(FILL[3 * i + 2])
                    pe.wait_ge(pT_ready, l * 4 + i + 1)
                    t = bank_free(pe, l, f"o{s}{g}")
                    for h in range(4):
                        hh = 4 * g + h
                        ins = mm(t[:, h * HD:(h + 1) * HD], pT[:, 0, h, :], v[:, s, hh * HD:(hh + 1) * HD],
                                 start=True, stop=not s)
                        if s:
                            ins = mm(t[:, h * HD:(h + 1) * HD], pT[:, 1, h, :], vctx[:, hh, :], start=False, stop=True)
                    fills(ins, f"o{s}{g}")
                fill(("gate", 0, 1, 0))
                branch_rows(l, 0, q)
                fill(("gate", 0, 1, 1))
                branch(l, 0)

                pe.wait_ge(ws_ready, l + 1)
                pe.wait_ge(gvn, l + 1)
                for s in range(2):
                    t = bank_free(pe, l, f"sp{s}")
                    for g in range(4):
                        ins = mm(t[:, g * P:(g + 1) * P], wsT[:, g, :], gv[:, s, g * P:(g + 1) * P], start=True, stop=True)
                    fills(ins, f"sp{s}")

                pe.wait_ge(dtA_ready, l + 1)
                for s in range(2):
                    t = bank_free(pe, l, f"ac{s}")
                    for i, m in enumerate(("upto", "since", "after", "before")):
                        r = i % 2
                        ins = mm(t[:, 8 * i:8 * i + 8], C[m], dtx[:, 9, s, 8 * r:8 * r + 8], start=True, stop=True)
                    fills(ins, f"ac{s}")
                pe.wait_ge(xbc_ready, 3 * l + 3)
                for s in range(2):
                    for g in range(2):
                        t = bank_free(pe, l, f"cb{s}{g}")
                        r = slice(g * HD, (g + 1) * HD)
                        ins = mm(t[:, 0:P], xbc[r, 4, s * P:(s + 1) * P], xbc[r, 5, s * P:(s + 1) * P], start=True, stop=True)
                        fills(ins, f"cb{s}{g}")
                    turn4(l, f"xs{s}", [xbc[:, m, s * P:(s + 1) * P] for m in range(4)])
                turn4(l, "bt", [xbc[:, 4, 0:P]])
                fill(GATES[2][0])
                pe.wait_ge(bt_ready, l + 1)
                for r in range(2):
                    pe.wait_ge(xw_ready, 2 * l + r + 1)
                    t = bank_free(pe, l, f"st{r}")
                    for h in range(HEADS):
                        ins = mm(t[0:HD, h * HD:(h + 1) * HD], xw[:, r, h * HD:(h + 1) * HD],
                                 btok[:, (h // 4) * HD:(h // 4 + 1) * HD], start=True, stop=True)
                    fills(ins, f"st{r}")
                for n in range(9):
                    if n < 8:
                        s, j = n // 4, n % 4
                        t = bank_free(pe, l, f"seg{n}")
                        for i in range(4):
                            h, r = 2 * j + i // 2, i % 2
                            ins = mm(t[:, i * P:(i + 1) * P], dtx[:, 9, s, 8 * r + h:8 * r + h + 1].to_broadcast([P, P]),
                                     C["upto" if r == 0 else "since"], start=True, stop=True)
                        fills(ins, f"seg{n}")
                    if 1 <= n < 8:
                        fill(SCAN_FILL[n - 1])
                    if n >= 1:
                        m = n - 1
                        s, j = m // 4, m % 4
                        if m == 0:
                            pe.wait_ge(xs_ready, 2 * l + 2)
                            pe.wait_ge(h0_ready, l + 1)
                        if j == 0:
                            yb = bank_free(pe, l, f"y{s}")
                        pe.wait_ge(W_ready, 8 * l + m + 1)
                        for i in range(4):
                            h, r = 2 * j + i // 2, i % 2
                            o = yb[:, h * HD:(h + 1) * HD]
                            ins = mm(o, W[:, m % 2, i, :], xs[:, s, h * HD:(h + 1) * HD], start=r == 0, stop=r == 1 and not s)
                            if s:
                                gp = slice((h // 4) * HD, (h // 4 + 1) * HD)
                                ins = mm(o, ctS[gp, m % 2, i, :], h0T[gp, r, h % 4, :], start=False, stop=r == 1)
                        if j == 3:
                            fills(ins, f"y{s}")
                            owed.append(y_sem)
                        else:
                            ins.then_inc(y_sem, 1)
                branch_rows(l, 2, u)
                branch(l, 2)
                branch_rows(l, 1, z)
                branch(l, 1)

                pe.wait_ge(merge_done, 3 * l + 3)
                for s in range(2):
                    mv = merged[:, s, :].rearrange("t (p c) -> t c p", c=DC)
                    for h in range(2):
                        turn4(l, f"mT{s}{h}", [mv[:, 4 * h + i, :] for i in range(4)])
                residual_rows(l, 2, "g1_")
                for s in range(2):
                    for h in range(2):
                        bank_free(pe, l, f"wo{s}{h}")
                pe.wait_ge(turned_low, l * 10 + 10)
                for i in range(4):
                    w = parts(l, ("wo", i), 1024)
                    for s in range(2):
                        for h in range(2):
                            for c in range(2):
                                ins = mm3(bank[2 * s + h][:, :], tokens(2 * i + c, s),
                                          [p[:, c, h * 512:(h + 1) * 512] for p in w], i == 0 and c == 0, i == 3 and c == 1)
                            if i == 3:
                                fills(ins, f"wo{s}{h}")
                    release(("wo", i))

                pe.wait_ge(x_ready, 2 * l + 2)
                turn_x(l, "x2T")
                pe.wait_ge(hT_ready, 2 * l + 2)
                w = parts(l, ("router",), 36)
                t = bank_free(pe, l, "rt")
                for s in range(2):
                    for c in range(DC):
                        ins = mm3(t[:, s * 36:s * 36 + 36], tokens(c, s), [p[:, c, :] for p in w], c == 0, c == DC - 1)
                fills(ins, "rt")
                release(("router",))
                for which, src in (("x2h", hTh), ("x2l", hTl)):
                    for s in range(2):
                        for h in range(2):
                            turn4(l, f"{which}{s}{h}", [src[:, 4 * h + i, s * P:(s + 1) * P].bitcast(F32) for i in range(4)])
                pe.wait_ge(onehot_ready, l + 1)
                t = bank_free(pe, l, "rank")
                one = [rtr[:, s, 8:12] for s in range(2)]
                mm(t[:, 0:4], C["before"], one[0], start=True, stop=True)
                mm(t[:, 4:8], C["upto"], one[0], start=True, stop=False)
                mm(t[:, 4:8], C["after"], one[0], start=False, stop=False)
                mm(t[:, 4:8], C["before"], one[1], start=False, stop=True)
                for s in range(2):
                    mm(t[:, 8:12], C["upto"], one[s], start=s == 0, stop=False)
                    ins = mm(t[:, 8:12], C["after"], one[s], start=False, stop=s == 1)
                fills(ins, "rank")

                pe.wait_ge(zero_ready, l + 1)
                zeros = tmp[:, 0:256].bitcast(BF16)
                for s in range(2):
                    for h in range(2):
                        t = bank_free(pe, l, f"moe{s}{h}")
                        mm(t[:, :], zeros[:, 0:P], zeros, start=True, stop=False, skip_group_check=True)
                pe.wait_ge(x2_ready, 8 * l + 8)

                def group(tally, rnd, g):
                    def loop_free(b, n):
                        pe.wait_ge(free[b], loop_uses(b, l, rnd, g, n))

                    def body_parts(key, **shape):
                        i = BODY.index(key)
                        pe.wait_ge(part_low[i % PARTS], N_PART.moe(l, rnd, g, i // PARTS + 1))
                        return [w[i % PARTS] for w in (wh, wl)]

                    pe.wait_ge(sel_ready, N_G.moe(l, rnd, g, 1))
                    for j, (b, src, h) in enumerate(((4, x2h, 0), (5, x2h, 1), (6, x2l, 0), (7, x2l, 1))):
                        loop_free(b, 0)
                        for i in range(4):
                            for s in range(2):
                                a = src[:, s, :].rearrange("t (p c) -> t c p", c=DC)[:, 4 * h + i, :]
                                ins = mm(bank[b][:, i * P:(i + 1) * P], a, selg[:, s, :], start=s == 0, stop=s == 1)
                        tally(ins, full[b])
                    loop_free(7, 1)
                    for s in range(2):
                        turn(bank[7][:, s * P:(s + 1) * P], selg[:, s, :].bitcast(F32), ident)
                    for s in range(2):
                        ins = mm(bank[7][:, 256:256 + EPG], selg[:, s, :].bitcast(F32), gsel[:, s, :], start=s == 0, stop=s == 1)
                    tally(ins, full[7])
                    pe.wait_ge(xg_act, N_G.moe(l, rnd, g, 1) * 2)
                    pe.wait_ge(xg_dve, N_G.moe(l, rnd, g, 1) * 2)

                    def up(e):
                        loop_free(UP_BANK, 1 + e)
                        o = bank[UP_BANK][:, :].rearrange("p (w f) -> p w f", w=2)
                        for h in range(2):
                            w = [p[:, :].rearrange("p (w c f) -> p c w f", w=2, c=4) for p in body_parts(("up", e, h))]
                            for c in range(4):
                                ins = mm3(o, [p[:, 4 * h + c, :] for p in (xgh, xgl)], [p[:, c] for p in w],
                                          h == 0 and c == 0, h == 1 and c == 3)
                            if h == 0:
                                owed.append(part_free[BODY.index(("up", e, 0)) % PARTS])
                                freed.append(part_free[BODY.index(("up", e, 0)) % PARTS])
                        tally(ins, full[UP_BANK])
                        owed.append(part_free[BODY.index(("up", e, 1)) % PARTS])
                        freed.append(part_free[BODY.index(("up", e, 1)) % PARTS])

                    def turn_hidden(e):
                        loop_free(TURN_BANK, 2 + e)
                        pe.wait_ge(hid_ready, N_E.moe(l, rnd, g, e + 1))
                        hv = hid[:, :].rearrange("t (p c) -> t c p", c=2)
                        for c in range(2):
                            ins = turn(bank[TURN_BANK][:, c * P:(c + 1) * P], hv[:, c, :], ident)
                        tally(ins, full[TURN_BANK])

                    def down(e):
                        w = [p[:, :].rearrange("p (c n) -> p c n", c=2) for p in body_parts(("down", e))]
                        pe.wait_ge(hidT_low, N_E.moe(l, rnd, g, e + 1))
                        for n in range(2):
                            if e == 0:
                                loop_free(SUM_BANK + n, 1)
                            for c in range(2):
                                ins = mm3(bank[SUM_BANK + n][:, :], [p[:, c, :] for p in (hTTh, hTTl)],
                                          [p[:, c, n * 512:(n + 1) * 512] for p in w], e == 0 and c == 0, e == EPG - 1 and c == 1)
                            if e == EPG - 1:
                                tally(ins, full[SUM_BANK + n])
                        owed.append(part_free[BODY.index(("down", e)) % PARTS])
                        freed.append(part_free[BODY.index(("down", e)) % PARTS])

                    freed = []
                    up(0)
                    turn_hidden(0)
                    for e in range(1, EPG):
                        up(e)
                        down(e - 1)
                        turn_hidden(e)
                    down(EPG - 1)
                    pe.wait_ge(selT_ready, N_G.moe(l, rnd, g, 1))
                    for n in range(2):
                        pe.wait_ge(yg_low, N_G.moe(l, rnd, g, 0) * 2 + (n + 1))
                        for s in range(2):
                            for yg in (ygh, ygl):
                                mm(bank[2 * s + n][:, :], selT[:, s, :], yg[:, n * 512:(n + 1) * 512], start=False, stop=False,
                                   skip_group_check=True)
                    for f in freed:
                        for i, t in enumerate(tally.sems):
                            if t is f:
                                tally.counts[i] += 1
                                break
                        else:
                            tally.sems.append(f)
                            tally.counts.append(1)

                rounds(pe, pe_waited, l, group, pe.drain)
                for s in range(2):
                    for h in range(2):
                        ins = mm(bank[2 * s + h][:, 0:2], zeros[:, 0:P], zeros[:, 0:2], start=False, stop=True, skip_group_check=True)
                        fills(ins, f"moe{s}{h}")
                residual_rows(l, 5, "g2_")

        @block.scalar
        def _(act):
            A_ = nc.scalar.activation
            act.wait_ge(once, 80)
            A_(tmp[:, 0:16].rearrange("p (s c) -> p s c", s=2), cs[:, :, :], ACT.Silu).then_inc(c_exp, 1)

            with act.Fori(0, L) as l:
                def convert_to(i):
                    while cut[0] <= i:
                        j = cut[0]
                        r, c = (RAW + j) % SLOTS, j % PARTS
                        n = min(PIECE, WIDTH[j])
                        act.wait_ge(slot_full[r], N_LOAD[r].mixer(l, LOAD_A[RAW + j]))
                        act.wait_ge(part_free[c], N_PART.mixer(l, j // PARTS + 1))
                        A_(wh[c][:, 0:n], raw[:, r, 0:n], ACT.Copy).then_inc(part_high[c], 1)
                        cut[0] += 1

                def ahead(key):
                    convert_to(min(SPLIT.index(key) + PARTS - 1, len(SPLIT) - 1))

                cut = [0]

                def modulate(sec, which, n):
                    if n == 0:
                        act.wait_ge(mod_ready, l + 1)
                    for h in range(2):
                        t = bank_full(act, l, f"{which}0{h}")
                        for i in range(4):
                            c = 4 * h + i
                            ins = A_(merged[:, 0, c * P:(c + 1) * P], t[:, i * P:(i + 1) * P], ACT.Identity,
                                     bias=mod[:, sec, c, 0:1], scale=mod[:, sec + 1, c, 0:1])
                        frees(ins, f"{which}0{h}")
                    act.drain()
                    for s in range(2):
                        if s:
                            act.wait_ge(hT_full, 2 * l + n + 1)
                        A_(hTh[:, :, s * P:(s + 1) * P], merged[:, s, :].rearrange("p (c t) -> p c t", c=DC),
                           ACT.Copy).then_inc(hT_high, 1)

                def take(name, dst, func, done, width=512, shape=None):
                    t = bank_full(act, l, name)
                    src = t[:, 0:width] if shape is None else shape(t)
                    frees(A_(dst, src, func), name)
                    if done is not None:
                        act.drain().then_inc(done, 1)

                def square_root(n):
                    act.wait_ge(var_ready, 4 * l + n + 1)
                    A_(root[:, :], root[:, :], ACT.Sqrt).then_inc(root_done, 1)

                for sec in range(N_ADA):
                    if sec >= 2:
                        act.wait_ge(ada_turned, l * (N_ADA - 1) + sec - 1)
                    for h in range(2):
                        t = bank_full(act, l, f"ada{sec}{h}")
                        frees(A_(merged[0:2, sec % 2, h * 512:(h + 1) * 512], t[0:2, :], ACT.Copy), f"ada{sec}{h}")
                    act.drain().then_inc(ada_rows, 1)
                convert_to(0)
                modulate(0, "x1T", 0)
                ahead(("q", 1))
                take("q0", q[:, 0, :], ACT.Copy, qv_act)
                ahead(("v", 1))
                act.wait_ge(stores_done, l + 1)
                take("v0", v[:, 0, :], ACT.Copy, qv_act)
                take("v1", v[:, 1, :], ACT.Copy, qv_act)

                def gate_take(b, n):
                    dst = gate1 if b == 1 else gate
                    if b == 2 and n == 0:
                        act.wait_ge(merge_done, 3 * l + 1)
                    if b == 1 and n == 0:
                        act.wait_ge(kv_stored, l + 1)
                    for s in range(2):
                        name = f"gate{b}{n}{s}"
                        t = bank_full(act, l, name)
                        frees(A_(dst[:, s, n * 512:(n + 1) * 512], t[:, :], ACT.Sigmoid), name)
                        act.drain().then_inc(gate_ready, 1)

                def branch_turned(b):
                    if b:
                        bank_full(act, l, f"br{ORDER[ORDER.index(b) - 1]}11")
                    for s in range(2):
                        t = bank_full(act, l, f"yT{b}{s}")
                        A_(yTh[:, :, s * P:(s + 1) * P], t[:, :].rearrange("p (c t) -> p c t", c=BC),
                           ACT.Copy).then_inc(turned_high, 1)

                def filled(n):
                    if n == 1:
                        for s in range(2):
                            take(f"z{s}", z[:, s, :], ACT.Silu, z_ready)
                    if n in (3, 5):
                        for m in ((0, 1) if n == 3 else (2,)):
                            act.wait_ge(conv_done, 3 * l + m + 1)
                            A_(xbc[:, 2 * m:2 * m + 2, :], xbc[:, 2 * m:2 * m + 2, :], ACT.Silu).then_inc(xbc_ready, 1)
                    if n == 6:
                        act.wait_ge(dt_in, l + 1)
                        A_(dtx[:, 2], dtx[:, 1], ACT.Exp, scale=-1.0)
                        A_(hrow[:, 16:32], hrow[:, 16:32], ACT.Exp)
                        act.drain()
                        A_(dtx[:, 3], dtx[:, 2], ACT.Ln, bias=1.0).then_inc(dt_ln, 1)
                    if n == 7:
                        for s in range(2):
                            take(f"u{s}", u[:, s, :], ACT.Gelu, gelu_u)
                    if n == 9:
                        for s in range(2):
                            take(f"gv{s}", gv[:, s, :], ACT.Gelu, gelu_v)
                    if n == 11:
                        gate_take(0, 0)

                ahead(FILL[0])
                for i, (s, g) in enumerate(UNITS):
                    ahead(FILL[3 * i])
                    act.wait_ge(smax, l * 4 + i + 1)
                    w = 2 * P if s else P
                    A_(S[:, :, 0:w], S[:, :, 0:w], ACT.Exp, scale=HD ** -0.5)
                    act.drain().then_inc(prob, 1)
                    filled(3 * i)
                    ahead(FILL[3 * i + 1])
                    filled(3 * i + 1)
                    for n, name in enumerate([f"pw{s}{g}"] + ([f"pc{g}"] if s else [])):
                        t = bank_full(act, l, name)
                        frees(A_(pT[:, n], t[:, :].rearrange("p (h t) -> p h t", h=4), ACT.Copy), name)
                    act.drain().then_inc(pT_ready, 1)
                    ahead(FILL[3 * i + 2])
                    filled(3 * i + 2)
                ahead(("gate", 0, 1, 0))
                branch_turned(0)
                ahead(("gate", 0, 1, 1))
                gate_take(0, 1)
                square_root(0)
                ahead(("branch", 0, 0))
                ahead(("branch", 0, 1))

                act.wait_ge(rem_ready, l + 1)
                A_(acs[:, 0, 16:32], acs[:, 0, 16:32], ACT.Exp).then_inc(rem_exp, 1)
                for s in range(2):
                    take(f"xs{s}", xs[:, s, :], ACT.Copy, xs_ready)
                ahead(GATES[2][0])
                for r in range(2):
                    if r == 0:
                        act.wait_ge(stores_done, l + 1)
                    t = bank_full(act, l, f"st{r}")
                    frees(A_(stout[:, r, :, :], t[0:HD, :].rearrange("p (h n) -> p h n", h=HEADS), ACT.Copy), f"st{r}")
                    act.drain().then_inc(st_ready, 1)
                for n in range(8):
                    if n >= 4:
                        t = bank_full(act, l, f"seg{n}")
                        if n >= 5:
                            act.wait_ge(ct_done, 4 * l + n - 4)
                        A_(eb[:, :, :], t[:, :].rearrange("p (i t) -> p i t", i=4), ACT.Exp)
                        act.drain().then_inc(eb_exp, 1)
                    act.wait_ge(seg_in, 8 * l + n + 1)
                    A_(seg[:, n % 2], seg[:, n % 2], ACT.Exp)
                    act.drain().then_inc(seg_exp, 1)
                    if n:
                        ahead(SCAN_FILL[n - 1])
                    if n in (2, 4, 6):
                        gate_take(*((2, 0), (2, 1), (1, 0))[n // 2 - 1])
                gate_take(1, 1)
                branch_turned(2)
                ahead(("branch", 2, 0))
                square_root(1)
                ahead(("branch", 2, 1))
                branch_turned(1)
                ahead(("branch", 1, 1))
                for s in range(2):
                    for h in range(2):
                        t = bank_full(act, l, f"mT{s}{h}")
                        A_(hTh[:, 4 * h:4 * h + 4, s * P:(s + 1) * P], t[:, :].rearrange("p (c t) -> p c t", c=4),
                           ACT.Copy).then_inc(turned_high, 1)
                ahead(("wo", 3))
                square_root(2)
                modulate(3, "x2T", 1)
                for n in range(2):
                    act.wait_ge(rt_in, 2 * l + n + 1)
                    w = rtr[:, :, 0:4] if n == 0 else rtr[:, :, 40:41]
                    A_(w, w, ACT.Exp).then_inc(rt_exp, 1)
                    if n == 0:
                        for s in range(2):
                            for h in range(2):
                                name = f"x2h{s}{h}"
                                t = bank_full(act, l, name)
                                frees(A_(x2h[:, s, :].rearrange("t (p c) -> t c p", c=DC)[:, 4 * h:4 * h + 4, :],
                                         t[:, :].rearrange("t (c p) -> t c p", c=4), ACT.Copy), name)
                                act.drain().then_inc(x2_ready, 1)

                def group(tally, rnd, g):
                    cut = [0]

                    def convert_to(i):
                        while cut[0] <= min(i, len(BODY) - 1):
                            j = cut[0]
                            r, c = j % SLOTS, j % PARTS
                            act.wait_ge(slot_full[r], N_LOAD[r].moe(l, rnd, g, LOAD_B[j]))
                            act.wait_ge(part_free[c], N_PART.moe(l, rnd, g, j // PARTS + 1))
                            tally(A_(wh[c][:, :], raw[:, r, :], ACT.Copy), part_high[c])
                            cut[0] += 1

                    convert_to(0)
                    for h in range(2):
                        act.wait_ge(full[4 + h], loop_uses(4 + h, l, rnd, g, 0))
                        tally(A_(xgh[:, 4 * h:4 * h + 4, :], bank[4 + h][:, :].rearrange("p (c t) -> p c t", c=4), ACT.Copy), free[4 + h])
                        tally(act.drain(), xg_act)
                    convert_to(2)
                    for e in range(EPG):
                        act.wait_ge(full[UP_BANK], loop_uses(UP_BANK, l, rnd, g, 1 + e))
                        act.wait_ge(free[UP_BANK], loop_uses(UP_BANK, l, rnd, g, 1 + e))
                        tally(A_(sil[:, :], bank[UP_BANK][:, 0:FF], ACT.Silu), sil_done)
                        convert_to(3 * e + 3)
                        act.wait_ge(full[TURN_BANK], loop_uses(TURN_BANK, l, rnd, g, 2 + e))
                        tally(A_(hTTh[:, :, :], bank[TURN_BANK][:, 0:FF].rearrange("p (c t) -> p c t", c=2), ACT.Copy), hidT_high)
                        convert_to(3 * e + 5)
                    for n in range(2):
                        act.wait_ge(full[SUM_BANK + n], loop_uses(SUM_BANK + n, l, rnd, g, 1))
                        tally(A_(ygh[:, n * 512:(n + 1) * 512], bank[SUM_BANK + n][:, :], ACT.Copy), yg_high)

                rounds(act, act_waited, l, group, act.drain)
                square_root(3)

        @block.vector
        def _(dve):
            V = nc.vector
            drain = dve.drain

            def tt(o, a, b, op):
                return V.tensor_tensor(o, a, b, op)

            for s in free + slot_free:
                dve.sem_inc(s, 1)
            dve.sem_inc(ln_used, 1)
            dve.wait_ge(once, 80)
            dve.sem_inc(x_ready, 1)
            dve.wait_ge(c_exp, 1)
            V.tensor_copy(cT[:, :, :].rearrange("p c s -> p s c"), tmp[:, 0:16].rearrange("p (s c) -> p s c", s=2)).then_inc(c_ready, 1)

            def inverse_root(l, n, var):
                V.tensor_scalar(root[:, :], var, EPS, None, ALU.add)
                drain().then_inc(var_ready, 1)
                dve.wait_ge(root_done, 4 * l + n + 1)
                V.reciprocal(root[:, :], root[:, :])
                drain()

            def layer_norm(l, n, t, width, g, b):
                blocks = width // 512
                for s in range(2):
                    for i in range(blocks):
                        V.bn_stats(stats[:, s, 6 * i:6 * i + 6], t[:, s, i * 512:(i + 1) * 512])
                drain()
                for s in range(2):
                    V.bn_aggr(mean_var[:, s, :], stats[:, s, 0:6 * blocks])
                drain()
                inverse_root(l, n, mean_var[:, :, 1])
                for s in range(2):
                    V.tensor_scalar(t[:, s, :], t[:, s, :], mean_var[:, s, 0:1], root[:, s:s + 1], ALU.subtract, ALU.mult)
                drain()
                tt(t[:, :, :], t[:, :, :], bc(g, 1, 2), ALU.mult)
                drain()
                tt(t[:, :, :], t[:, :, :], bc(b, 1, 2), ALU.add)

            with dve.Fori(0, L) as l:
                def convert_to(i):
                    while cut[0] <= i:
                        j = cut[0]
                        r, c = (RAW + j) % SLOTS, j % PARTS
                        n = min(PIECE, WIDTH[j])
                        dve.wait_ge(part_high[c], N_PART.mixer(l, j // PARTS + 1))
                        tt(wl[c][:, 0:n], raw[:, r, 0:n], wh[c][:, 0:n].bitcast(F32), ALU.subtract).then_inc(part_low[c], 1)
                        drain().then_inc(slot_free[r], 1)
                        cut[0] += 1

                def ahead(key):
                    convert_to(min(SPLIT.index(key) + PARTS - 1, len(SPLIT) - 1))

                cut = [0]

                def modulate(sec, which, n):
                    for h in range(2):
                        t = bank_full(dve, l, f"{which}1{h}")
                        for i in range(4):
                            c = 4 * h + i
                            ins = V.tensor_scalar(merged[:, 1, c * P:(c + 1) * P], t[:, i * P:(i + 1) * P],
                                                  mod[:, sec + 1, c, 1:2], mod[:, sec, c, 1:2], ALU.mult, ALU.add)
                        frees(ins, f"{which}1{h}")
                    drain().then_inc(hT_full, 1)
                    for s in range(2):
                        dve.wait_ge(hT_high, 4 * l + 2 * n + s + 1)
                        tt(hTl[:, :, s * P:(s + 1) * P], merged[:, s, :].rearrange("p (c t) -> p c t", c=DC),
                           hTh[:, :, s * P:(s + 1) * P].bitcast(F32), ALU.subtract)
                    drain().then_inc(hT_ready, 1)

                def turned(b, name, high, low):
                    t = bank_full(dve, l, name)
                    dve.wait_ge(turned_high, l * 10 + b + 1)
                    frees(tt(low, t[:, :].rearrange("p (c t) -> p c t", c=4), high.bitcast(F32), ALU.subtract), name)
                    drain().then_inc(turned_low, 1)

                def branch_turned(b):
                    for s in range(2):
                        cols_ = slice(s * P, (s + 1) * P)
                        turned(2 * ORDER.index(b) + s, f"yT{b}{s}", yTh[:, :, cols_], yTl[:, :, cols_])

                def residual_rows(which):
                    for s in range(2):
                        for h in range(2):
                            t = bank_full(dve, l, f"{which}{s}{h}")
                            gs = gate[:, s, :].rearrange("t (p c) -> t c p", c=DC)[:, 4 * h:4 * h + 4, :]
                            frees(V.tensor_copy(gs, t[:, :].rearrange("t (c p) -> t c p", c=4)), f"{which}{s}{h}")
                    drain()

                def residual(out, n):
                    dve.wait_ge(lnload, (2 * l + n + 1) * 16)
                    bank_full(dve, l, f"{out}11")
                    for s in range(2):
                        for h in range(2):
                            t = bank_full(dve, l, f"{out}{s}{h}")
                            frees(tt(tmp[:, h * 512:(h + 1) * 512], t[:, :], gate[:, s, h * 512:(h + 1) * 512], ALU.mult), f"{out}{s}{h}")
                        drain()
                        V.scalar_tensor_tensor(out=x[:, s, :], in0=x[:, s, :], scalar=ALPHA, in1=tmp[:, :], op0=ALU.mult, op1=ALU.add)
                        drain()
                    layer_norm(l, 2 + n, x, D, lnrow[:, 0, :], lnrow[:, 1, :])

                dve.wait_ge(params, (l + 1) * 16 * N_PARAM)
                t = bank_full(dve, l, "ada")
                frees(tt(mod[:, :, :, :].rearrange("p a c s -> p (a c) s"), t[:, 0:96].rearrange("p (a s) -> p a s", s=2),
                         bc(bada[:, :, :].rearrange("p a c -> p (a c)"), 2, 2), ALU.add), "ada")
                drain()
                for sec in (1, 4):
                    V.tensor_scalar(mod[:, sec], mod[:, sec], 1.0, None, ALU.add)
                drain().then_inc(mod_ready, 1)
                t = bank_full(dve, l, "rows")
                frees(V.tensor_copy(cols[:, :], t[:, 0:28]), "rows")
                t = bank_full(dve, l, "ws")
                frees(V.tensor_copy(wsT[:, :, :], t[:, :].rearrange("p (g i) -> p g i", g=4)), "ws")
                drain().then_inc(ws_ready, 1)
                t = bank_full(dve, l, "h0")
                frees(V.tensor_copy(h0T[:, :, :, :].rearrange("p r j n -> p (r j n)"), t[:, :]), "h0")
                drain().then_inc(h0_ready, 1)
                convert_to(0)
                modulate(0, "x1T", 0)

                def rope(name, dst):
                    t = bank_full(dve, l, name)
                    t3 = t[:, :].rearrange("t (h d) -> t h d", h=HEADS)
                    cos = bc(C["cos"], 1, HEADS)
                    tt(dst.rearrange("t (h d) -> t h d", h=HEADS), t3, cos, ALU.mult)
                    t5 = t[:, :].rearrange("t (a b i) -> t a b i", b=2, i=16)
                    r5 = ropet[:, :].rearrange("t (a b i) -> t a b i", b=2, i=16)
                    V.tensor_copy(r5[:, :, 0, :], t5[:, :, 1, :])
                    frees(V.tensor_copy(r5[:, :, 1, :], t5[:, :, 0, :]), name)
                    drain()
                    r3 = ropet[:, :].rearrange("t (h d) -> t h d", h=HEADS)
                    tt(r3, r3, bc(C["sin"], 1, HEADS), ALU.mult)
                    drain()
                    tt(dst, dst, ropet[:, :], ALU.add)
                    drain().then_inc(qk_dve, 1)

                ahead(("q", 1))
                rope("q1", q[:, 1, :])
                ahead(("k", 1))
                dve.wait_ge(stores_done, l + 1)
                t = bank_full(dve, l, "k0")
                frees(V.tensor_copy(k[:, 0, :], t[:, :]), "k0")
                drain().then_inc(qk_dve, 1)
                rope("k1", k[:, 1, :])

                def convolve(m):
                    t = bank_full(dve, l, f"xbc{m}")
                    for i in range(2):
                        ch = 2 * m + i
                        src = t[:, i * 256:(i + 1) * 256]
                        s3 = src.rearrange("p (s t) -> p s t", s=2)
                        o3 = xbc[:, ch, :].rearrange("p (s t) -> p s t", s=2)
                        V.tensor_scalar(xbc[:, ch, :], src, cols[:, 6 + ch:7 + ch], cols[:, 18 + ch:19 + ch], ALU.mult, ALU.add)
                        drain()
                        V.scalar_tensor_tensor(out=o3[:, :, 1:P], in0=s3[:, :, 0:P - 1], scalar=cols[:, ch:ch + 1],
                                               in1=o3[:, :, 1:P], op0=ALU.mult, op1=ALU.add)
                        drain()
                        ins = V.scalar_tensor_tensor(out=o3[:, :, 0:P - 1], in0=s3[:, :, 1:P], scalar=cols[:, 12 + ch:13 + ch],
                                                     in1=o3[:, :, 0:P - 1], op0=ALU.mult, op1=ALU.add)
                    frees(ins, f"xbc{m}")
                    drain().then_inc(conv_done, 1)

                def step_in():
                    t = bank_full(dve, l, "dt")
                    frees(tt(dtx[:, 0], t[:, 0:32].rearrange("p (s h) -> p s h", s=2), bc(hrow[:, 0:16], 1, 2), ALU.add), "dt")
                    drain()
                    V.scalar_tensor_tensor(out=dtx[:, 1], in0=dtx[:, 0], scalar=-1.0, in1=dtx[:, 0], op0=ALU.mult, op1=ALU.max)
                    drain().then_inc(dt_in, 1)

                def gv_norm():
                    dve.wait_ge(gelu_v, 2 * l + 2)
                    layer_norm(l, 0, gv, NW, rows3[:, 0, :], rows3[:, 1, :])
                    drain().then_inc(gvn, 1)

                def steps():
                    dve.wait_ge(dt_ln, l + 1)
                    V.tensor_scalar(dtx[:, 4], dtx[:, 2], 1.0, None, ALU.add)
                    V.tensor_scalar(dtx[:, 5], dtx[:, 3], TINY, None, ALU.add)
                    V.tensor_scalar(dtx[:, 6], dtx[:, 0], 0.0, None, ALU.max)
                    drain()
                    V.tensor_scalar(dtx[:, 4], dtx[:, 4], -1.0, TINY, ALU.add, ALU.add)
                    tt(dtx[:, 5], dtx[:, 5], dtx[:, 2], ALU.mult)
                    drain()
                    V.reciprocal(dtx[:, 4], dtx[:, 4])
                    drain()
                    tt(dtx[:, 5], dtx[:, 5], dtx[:, 4], ALU.mult)
                    drain()
                    tt(dtx[:, 8], dtx[:, 5], dtx[:, 6], ALU.add)
                    drain()
                    V.scalar_tensor_tensor(out=dtx[:, 9], in0=dtx[:, 8], scalar=-1.0, in1=bc(hrow[:, 16:32], 1, 2),
                                           op0=ALU.mult, op1=ALU.mult)
                    drain().then_inc(dtA_ready, 1)

                def filled(n):
                    if n == 3:
                        convolve(0)
                        convolve(1)
                    if n == 5:
                        convolve(2)
                        step_in()
                    if n == 10:
                        steps()

                def merge(b):
                    dve.wait_ge(gate_ready, l * 12 + 4 * ORDER.index(b) + 4)
                    gates_ = gate1 if b == 1 else gate
                    for h in range(2):
                        hs = slice(h * 512, (h + 1) * 512)
                        for s in range(2):
                            t = bank_full(dve, l, f"br{b}{h}{s}")
                            out = merged[:, s, hs] if b == 0 else tmp[:, s * 512:(s + 1) * 512]
                            frees(tt(out, t[:, :], gates_[:, s, hs], ALU.mult), f"br{b}{h}{s}")
                        if b:
                            drain()
                            tt(merged[:, :, hs], merged[:, :, hs], tmp[:, :].rearrange("t (s n) -> t s n", s=2), ALU.add)
                            drain()
                    drain().then_inc(merge_done, 1)

                ahead(FILL[0])
                for i, (s, g) in enumerate(UNITS):
                    for dst, name in [(qT, f"qT{s}{g}"), (kT, f"kT{s}{g}")] + ([(cTk, f"cT{g}")] if s else []):
                        t = bank_full(dve, l, name)
                        frees(V.tensor_copy(dst[:, :, :], t[0:HD, :].rearrange("p (h t) -> p h t", h=4)), name)
                        drain().then_inc(qkT_dve, 1)
                    ahead(FILL[3 * i])
                    w = P
                    t = bank_full(dve, l, f"sw{s}{g}")
                    t3 = t[:, :].rearrange("t (h k) -> t h k", h=4)
                    if i:
                        bank_full(dve, l, f"pc{g - 1}" if s and g else f"pw{0}{1}" if s else "pw00")
                    if s:
                        w = 2 * P
                        V.scalar_tensor_tensor(out=S[:, :, P:2 * P], in0=bias[:, 4 * g:4 * g + 4, :], scalar=HD ** 0.5,
                                               in1=bc(C["window"], 1, 4), op0=ALU.mult, op1=ALU.add)
                        drain()
                        frees(tt(S[:, :, 0:P], t3, S[:, :, P:2 * P], ALU.add), f"sw{s}{g}")
                        drain()
                        t = bank_full(dve, l, f"sc{g}")
                        frees(V.tensor_copy(S[:, :, P:2 * P], t[:, :].rearrange("t (h k) -> t h k", h=4)), f"sc{g}")
                        drain()
                        V.tensor_reduce(small[:, 20:24], S[:, :, :], X, ALU.max)
                        drain()
                        tt(S[:, :, :], S[:, :, :], bc(small[:, 20:24], 2, w), ALU.subtract)
                    else:
                        V.tensor_reduce(small[:, 20:24], t3, X, ALU.max)
                        drain()
                        frees(tt(S[:, :, 0:P], t3, bc(small[:, 20:24], 2, w), ALU.subtract), f"sw{s}{g}")
                    drain().then_inc(smax, 1)
                    filled(3 * i)
                    ahead(FILL[3 * i + 1])
                    dve.wait_ge(prob, l * 4 + i + 1)
                    V.tensor_reduce(small[:, 24:28], S[:, :, 0:w], X, ALU.add)
                    drain()
                    V.reciprocal(small[:, 28:32], small[:, 24:28])
                    drain()
                    filled(3 * i + 1)
                    ahead(FILL[3 * i + 2])
                    t = bank_full(dve, l, f"o{s}{g}")
                    frees(tt(q[:, s, g * 256:(g + 1) * 256].rearrange("t (h d) -> t h d", h=4),
                             t[:, 0:256].rearrange("t (h d) -> t h d", h=4), bc(small[:, 28:32], 2, HD), ALU.mult), f"o{s}{g}")
                    if i == 3:
                        drain().then_inc(y_ready[0], 1)
                    filled(3 * i + 2)
                ahead(("gate", 0, 1, 0))
                branch_turned(0)
                ahead(("gate", 0, 1, 1))
                gv_norm()
                ahead(("branch", 0, 0))
                ahead(("branch", 0, 1))
                merge(0)

                dve.wait_ge(gelu_u, 2 * l + 2)
                for s in range(2):
                    t = bank_full(dve, l, f"sp{s}")
                    for g in range(4):
                        gs = slice(g * P, (g + 1) * P)
                        ins = V.scalar_tensor_tensor(out=u[:, s, gs], in0=t[:, gs], scalar=cols[:, 24 + g:25 + g],
                                                     in1=u[:, s, gs], op0=ALU.add, op1=ALU.mult)
                    frees(ins, f"sp{s}")
                drain().then_inc(y_ready[2], 1)

                for s in range(2):
                    t = bank_full(dve, l, f"ac{s}")
                    frees(V.tensor_copy(acs[:, s, :], t[:, 0:32]), f"ac{s}")
                drain().then_inc(rem_ready, 1)

                def cb_of(s):
                    for g in range(2):
                        t = bank_full(dve, l, f"cb{s}{g}")
                        frees(V.tensor_copy(cbraw[:, s, g, :], t[:, 0:P]), f"cb{s}{g}")

                cbraw = ropet[:, :].rearrange("p (s g t) -> p s g t", s=2, g=2)
                for s in range(2):
                    cb_of(s)
                t = bank_full(dve, l, "bt")
                frees(V.tensor_copy(btok[:, :], t[:, 0:P]), "bt")
                drain().then_inc(bt_ready, 1)
                ahead(GATES[2][0])
                dve.wait_ge(rem_exp, l + 1)
                tt(wend[:, :], acs[:, 0, 16:32], dtx[:, 8, 0, :], ALU.mult)
                drain()
                dve.wait_ge(xs_ready, 2 * l + 2)
                for r in range(2):
                    tt(xw[:, r, :].rearrange("t (h d) -> t h d", h=HEADS), xs[:, 0, :].rearrange("t (h d) -> t h d", h=HEADS),
                       bc(wend[:, 8 * r:8 * r + 8], 2, HD), ALU.mult)
                    drain().then_inc(xw_ready, 1)
                for n in range(9):
                    if n < 8:
                        s, j = n // 4, n % 4
                        if n in (0, 1):
                            bank_full(dve, l, f"st{n}")
                        if n >= 4:
                            dve.wait_ge(eb_exp, 4 * l + n - 3)
                        t = bank_full(dve, l, f"seg{n}")
                        for i in range(4):
                            h, r = 2 * j + i // 2, i % 2
                            ins = V.tensor_scalar(seg[:, n % 2, i, :], t[:, i * P:(i + 1) * P],
                                                  acs[:, s, 8 * r + h:8 * r + h + 1], 0.0, ALU.subtract, ALU.min)
                        frees(ins, f"seg{n}")
                        drain().then_inc(seg_in, 1)
                        if n >= 4:
                            gp = slice((j // 2) * HD, (j // 2 + 1) * HD)
                            dve.wait_ge(y_sem, 8 * l + n - 1)
                            tt(ctS[gp, n % 2], eb[gp], bc(xbc[gp, 5, P:2 * P], 1, 4), ALU.mult).then_inc(ct_done, 1)
                    if n >= 1:
                        m = n - 1
                        s, j = m // 4, m % 4
                        if m % 4 == 0:
                            for r, mask in enumerate(("upto", "since")):
                                tt(cbm[:, r], cbraw[:, s], bc(C[mask], 1, 2), ALU.mult)
                            drain()
                        dve.wait_ge(seg_exp, 8 * l + m + 1)
                        if m >= 2:
                            dve.wait_ge(y_sem, 8 * l + m - 1)
                        for i in range(4):
                            h, r = 2 * j + i // 2, i % 2
                            V.scalar_tensor_tensor(out=W[:, m % 2, i, :], in0=seg[:, m % 2, i, :],
                                                   scalar=dtx[:, 8, s, 8 * r + h:8 * r + h + 1], in1=cbm[:, r, h // 4, :],
                                                   op0=ALU.mult, op1=ALU.mult)
                        drain().then_inc(W_ready, 1)
                    if 1 <= n < 8:
                        ahead(SCAN_FILL[n - 1])
                branch_turned(2)
                dve.wait_ge(z_ready, 2 * l + 2)
                for s in range(2):
                    y = tmp[:, 0:NW]
                    tt(y.rearrange("t (h d) -> t h d", h=HEADS), xs[:, s, :].rearrange("t (h d) -> t h d", h=HEADS),
                       bc(hrow[:, 32:40], 2, HD), ALU.mult)
                    drain()
                    t = bank_full(dve, l, f"y{s}")
                    frees(tt(y, t[:, :], y, ALU.add), f"y{s}")
                    drain()
                    tt(z[:, s, :], y, z[:, s, :], ALU.mult)
                    drain()
                    tt(tmp[:, NW:D], z[:, s, :], z[:, s, :], ALU.mult)
                    drain()
                    V.tensor_reduce(small[:, s:s + 1], tmp[:, NW:D], X, ALU.add)
                    drain()
                V.tensor_scalar(small[:, 2:4], small[:, 0:2], 1.0 / NW, None, ALU.mult)
                drain()
                inverse_root(l, 1, small[:, 2:4])
                for s in range(2):
                    V.scalar_tensor_tensor(out=z[:, s, :], in0=z[:, s, :], scalar=root[:, s:s + 1], in1=rows3[:, 2, :],
                                           op0=ALU.mult, op1=ALU.mult)
                drain().then_inc(y_ready[1], 1)
                ahead(("branch", 2, 1))
                merge(2)
                branch_turned(1)
                ahead(("branch", 1, 1))
                merge(1)
                for s in range(2):
                    for h in range(2):
                        part = (slice(None), slice(4 * h, 4 * h + 4), slice(s * P, (s + 1) * P))
                        turned(6 + 2 * s + h, f"mT{s}{h}", hTh[part], hTl[part])
                residual_rows("g1_")
                ahead(("wo", 3))
                residual("wo", 0)
                drain().then_inc(x_ready, 1)
                dve.sem_inc(ln_used, 1)

                V.memset(tmp[:, 0:512], 0.0)
                drain().then_inc(zero_ready, 1)
                modulate(3, "x2T", 1)
                t = bank_full(dve, l, "rt")
                frees(V.tensor_copy(lg[:, :, :], t[:, 0:72].rearrange("p (s n) -> p s n", s=2)), "rt")
                drain()

                def r_(a, b):
                    return rtr[:, :, a:b]

                V.tensor_reduce(r_(4, 5), lg[:, :, 0:4], X, ALU.max)
                drain()
                tt(r_(0, 4), lg[:, :, 0:4], r_(4, 5).to_broadcast([P, 2, 4]), ALU.subtract)
                tt(r_(8, 12), lg[:, :, 0:4], r_(4, 5).to_broadcast([P, 2, 4]), ALU.is_equal)
                drain().then_inc(rt_in, 1)

                def first(a, n, rev, m):
                    tt(r_(a, a + n), r_(a, a + n), bc(C[rev], 1, 2), ALU.mult)
                    drain()
                    V.tensor_reduce(r_(m, m + 1), r_(a, a + n), X, ALU.max)
                    drain()
                    tt(r_(a, a + n), r_(a, a + n), r_(m, m + 1).to_broadcast([P, 2, n]), ALU.is_equal)
                    drain()

                first(8, 4, "rev4", 5)
                dve.sem_inc(onehot_ready, 1)
                for s in range(2):
                    for h in range(2):
                        name = f"x2l{s}{h}"
                        t = bank_full(dve, l, name)
                        frees(V.tensor_copy(x2l[:, s, :].rearrange("t (p c) -> t c p", c=DC)[:, 4 * h:4 * h + 4, :],
                                            t[:, :].rearrange("t (c p) -> t c p", c=4)), name)
                        drain().then_inc(x2_ready, 1)
                for s in range(2):
                    tt(tmp[:, 512 + 32 * s:544 + 32 * s].rearrange("p (e g) -> p e g", g=4),
                       lg[:, s, 4:36].rearrange("p (g e) -> p e g", g=4), bc(rtr[:, s, 8:12], 1, 8), ALU.mult)
                drain()
                V.tensor_reduce(r_(16, 24), tmp[:, 512:576].rearrange("p (s e g) -> p s e g", s=2, g=4), X, ALU.add)
                drain()
                V.tensor_reduce(r_(6, 7), r_(16, 24), X, ALU.max)
                drain()
                tt(r_(24, 32), r_(16, 24), r_(6, 7).to_broadcast([P, 2, 8]), ALU.is_equal)
                drain()
                first(24, 8, "rev8", 5)
                V.scalar_tensor_tensor(out=r_(16, 24), in0=r_(24, 32), scalar=-BIG, in1=r_(16, 24), op0=ALU.mult, op1=ALU.add)
                drain()
                V.tensor_reduce(r_(7, 8), r_(16, 24), X, ALU.max)
                drain()
                tt(r_(32, 40), r_(16, 24), r_(7, 8).to_broadcast([P, 2, 8]), ALU.is_equal)
                tt(r_(40, 41), r_(7, 8), r_(6, 7), ALU.subtract)
                drain().then_inc(rt_in, 1)
                first(32, 8, "rev8", 5)
                dve.wait_ge(rt_exp, 2 * l + 2)
                V.tensor_reduce(r_(41, 42), r_(0, 4), X, ALU.add)
                V.tensor_scalar(r_(42, 43), r_(40, 41), 1.0, None, ALU.add)
                drain()
                tt(r_(43, 44), r_(41, 42), r_(42, 43), ALU.mult)
                drain()
                V.reciprocal(r_(44, 45), r_(43, 44))
                drain()
                tt(r_(45, 46), r_(44, 45), r_(40, 41), ALU.mult)
                drain()
                tt(r_(24, 32), r_(24, 32), r_(44, 45).to_broadcast([P, 2, 8]), ALU.mult)
                tt(r_(32, 40), r_(32, 40), r_(45, 46).to_broadcast([P, 2, 8]), ALU.mult)
                drain()
                tt(r_(24, 32), r_(24, 32), r_(32, 40), ALU.add)
                drain()
                for s in range(2):
                    tt(gates[:, s, :].rearrange("p (g e) -> p g e", g=4), bc(rtr[:, s, 24:32], 1, 4), bc(rtr[:, s, 8:12], 2, 8), ALU.mult)
                drain()
                t = bank_full(dve, l, "rank")
                frees(V.tensor_copy(rank[:, 0:12], t[:, 0:12]), "rank")
                drain()
                tt(rank[:, 0:8].rearrange("p (s g) -> p s g", s=2), rank[:, 0:8].rearrange("p (s g) -> p s g", s=2), r_(8, 12), ALU.mult)
                V.tensor_reduce(rank[:, 12:13], rank[:, 8:12], X, ALU.max)
                drain()
                V.tensor_reduce(place[:, :, 0:1], rank[:, 0:8].rearrange("p (s g) -> p s g", s=2), X, ALU.add)
                V.tensor_scalar(need[0:1, 0:1], rank[0:1, 12:13], float(P), None, ALU.is_gt)
                drain()
                V.tensor_scalar(place[:, :, 1:2], place[:, :, 0:1], -float(P), None, ALU.add)
                drain().then_inc(need_ready, 1)

                def group(tally, rnd, g):
                    cut = [0]

                    def convert_to(i):
                        while cut[0] <= min(i, len(BODY) - 1):
                            j = cut[0]
                            r, c = j % SLOTS, j % PARTS
                            dve.wait_ge(part_high[c], N_PART.moe(l, rnd, g, j // PARTS + 1))
                            tally(tt(wl[c][:, :], raw[:, r, :], wh[c][:, :].bitcast(F32), ALU.subtract), part_low[c])
                            tally(drain(), slot_free[r])
                            cut[0] += 1

                    for s in range(2):
                        V.tensor_scalar(selg[:, s, :], C["iota"], place[:, s, rnd:rnd + 1], rtr[:, s, bass.ds(g + 8, 1)],
                                        ALU.is_equal, ALU.mult)
                    V.tensor_copy(gsel[:, :, :], gates[:, :, bass.ds(g * EPG, EPG)])
                    tally(drain(), sel_ready)
                    convert_to(0)
                    for h in range(2):
                        b = 6 + h
                        dve.wait_ge(full[b], loop_uses(b, l, rnd, g, 0))
                        tally(V.tensor_copy(xgl[:, 4 * h:4 * h + 4, :], bank[b][:, :].rearrange("p (c t) -> p c t", c=4)), free[b])
                        tally(drain(), xg_dve)
                    dve.wait_ge(full[7], loop_uses(7, l, rnd, g, 1))
                    V.tensor_copy(gg[:, :], bank[7][:, 256:256 + EPG])
                    tally(V.tensor_copy(selT[:, :, :], bank[7][:, 0:256].rearrange("p (s t) -> p s t", s=2)), free[7])
                    tally(drain(), selT_ready)
                    convert_to(2)
                    for e in range(EPG):
                        dve.wait_ge(full[UP_BANK], loop_uses(UP_BANK, l, rnd, g, 1 + e))
                        dve.wait_ge(sil_done, N_E.moe(l, rnd, g, e + 1))
                        if e:
                            dve.wait_ge(full[TURN_BANK], loop_uses(TURN_BANK, l, rnd, g, 1 + e))
                        tally(V.scalar_tensor_tensor(out=hid[:, :], in0=bank[UP_BANK][:, FF:2 * FF], scalar=gg[:, e:e + 1],
                                                     in1=sil[:, :], op0=ALU.mult, op1=ALU.mult), free[UP_BANK])
                        tally(drain(), hid_ready)
                        convert_to(3 * e + 3)
                        dve.wait_ge(full[TURN_BANK], loop_uses(TURN_BANK, l, rnd, g, 2 + e))
                        dve.wait_ge(hidT_high, N_E.moe(l, rnd, g, e + 1))
                        tally(tt(hTTl[:, :, :], bank[TURN_BANK][:, 0:FF].rearrange("p (c t) -> p c t", c=2),
                                 hTTh[:, :, :].bitcast(F32), ALU.subtract), free[TURN_BANK])
                        tally(drain(), hidT_low)
                        convert_to(3 * e + 5)
                    for n in range(2):
                        dve.wait_ge(full[SUM_BANK + n], loop_uses(SUM_BANK + n, l, rnd, g, 1))
                        dve.wait_ge(yg_high, N_G.moe(l, rnd, g, 0) * 2 + (n + 1))
                        tally(tt(ygl[:, n * 512:(n + 1) * 512], bank[SUM_BANK + n][:, :],
                                 ygh[:, n * 512:(n + 1) * 512].bitcast(F32), ALU.subtract), free[SUM_BANK + n])
                        tally(drain(), yg_low)

                rounds(dve, dve_waited, l, group, dve.drain)
                bank_full(dve, l, "moe11")
                residual_rows("g2_")
                residual("moe", 1)
                drain().then_inc(x_ready, 1)
                dve.sem_inc(ln_used, 1)
                dve.sem_inc(out_ready, 1)


_SHAPES = dict(y_prompt=(1, P, D), y_sample=(1, P, D), new_k=(1, L, HEADS, P, HD), new_v=(1, L, HEADS, P, HD),
               new_state=(1, L, 2, HEADS, HD, HD))


def kernel(**inputs):
    import numpy as _np
    import concourse.bacc as _bacc
    from concourse import mybir as _mybir
    from concourse.bass_utils import run_bass_kernel_spmd as _run

    a = {n: _np.ascontiguousarray(w) for n, w in inputs.items()}
    a["router"] = _np.concatenate([a.pop("moe_w_coarse"), a.pop("moe_w_fine")], 2)
    a["chan_rows"] = _np.concatenate([a.pop("ssm_conv_w").reshape(L, 18, P), a.pop("ssm_conv_b").reshape(L, 6, P), a.pop("gmlp_bs")], 1)
    a["head_rows"] = _np.concatenate([a.pop("ssm_dt_bias").reshape(L, 16), a.pop("ssm_a_log").reshape(L, 16), a.pop("ssm_d")], 1)
    a["rows3"] = _np.stack([a.pop("gmlp_ln_g"), a.pop("gmlp_ln_b"), a.pop("ssm_norm_g")], 1)
    a["ln_rows"] = _np.stack([a.pop("ln_g"), a.pop("ln_b")], 2)
    a["consts"] = const_array()
    nc = _bacc.Bacc("TRN2", target_bir_lowering=False, num_devices=1)
    arrays, ins, outs = {}, {}, {}
    for name, w in a.items():
        arrays[f"in_{name}"] = w
        ins[name] = nc.dram_tensor(f"in_{name}", w.shape, _mybir.dt.from_np(w.dtype), kind="ExternalInput").ap()
    for name, shape in _SHAPES.items():
        outs[name] = nc.dram_tensor(f"out_{name}", shape, F32, kind="ExternalOutput").ap()
    hybrid_backbone(nc, ins, outs)
    r = _run(nc, [arrays], core_ids=[0])
    return tuple(r.results[0][f"out_{name}"] for name in _SHAPES)
```
